# Optimizing a Trainium2 kernel written in Bass

```python
import jax
import jax.numpy as jnp
from jax import lax
import numpy as np

D_MODEL = 1024
BATCH = 1
SEQ = 256
DEPTH = 2

GRID_W = 64
CTX_LEN = 256
HEAD_DIM = 64
N_Q_HEADS = 12
N_KV_HEADS = 4
Q_PER_KV = N_Q_HEADS // N_KV_HEADS
ATTN_WIDTH = N_Q_HEADS * HEAD_DIM
KV_WIDTH = N_KV_HEADS * HEAD_DIM
N_FOURIER_GROUPS = 4
FOURIER_GROUP_DIM = 64
FOURIER_WIDTH = N_FOURIER_GROUPS * FOURIER_GROUP_DIM
MIX_WIDTH = ATTN_WIDTH + FOURIER_WIDTH
EVEN_IN_WIDTH = ATTN_WIDTH + 2 * KV_WIDTH + FOURIER_WIDTH
EVEN_SPLITS = (ATTN_WIDTH, ATTN_WIDTH + KV_WIDTH, ATTN_WIDTH + 2 * KV_WIDTH)
CONV_WIDTH = D_MODEL
CONV_K = 3
D_FF = 2816
N_EXPERTS = 8
TOP_K = 2
D_EXPERT = 3584
Q_BLOCK = 128
ROPE_THETA = 10000.0
ROPE_AXIS_DIM = HEAD_DIM // 2
NORM_EPS = 1e-6
N_EVEN = (DEPTH + 1) // 2
N_ODD = DEPTH // 2

kernel_name = 'hybrid_fourier_gqa_shortconv_moe_dit'

def rmsnorm(x, g):
    xf = x.astype(jnp.float32)
    y = xf * lax.rsqrt(jnp.mean(xf * xf, axis=-1, keepdims=True) + NORM_EPS)
    return (y * g.astype(jnp.float32)).astype(x.dtype)

def modulate(x, g, shift, scale):
    return rmsnorm(x, g) * (1 + scale) + shift

def axial_rope_angles(n_tokens):
    rows = n_tokens // GRID_W
    row = jnp.repeat(jnp.arange(rows, dtype=jnp.float32), GRID_W)
    col = jnp.tile(jnp.arange(GRID_W, dtype=jnp.float32), rows)
    half = ROPE_AXIS_DIM // 2
    inv_freq = ROPE_THETA ** (-jnp.arange(half, dtype=jnp.float32) / half)
    return row[:, None] * inv_freq, col[:, None] * inv_freq

def rotate_axis(x, ang):
    cos = jnp.cos(ang)[None, :, None, :]
    sin = jnp.sin(ang)[None, :, None, :]
    x1, x2 = jnp.split(x, 2, axis=-1)
    return jnp.concatenate([x1 * cos - x2 * sin, x1 * sin + x2 * cos], axis=-1)

def rope_2d(x, ang_row, ang_col):
    xf = x.astype(jnp.float32)
    out = jnp.concatenate([rotate_axis(xf[..., :ROPE_AXIS_DIM], ang_row),
                           rotate_axis(xf[..., ROPE_AXIS_DIM:], ang_col)], axis=-1)
    return out.astype(x.dtype)

def heads(t, n):
    return t.reshape(t.shape[0], t.shape[1], n, HEAD_DIM)

def gqa_attend(q, k, v):
    b, lq = q.shape[0], q.shape[1]
    n_blk = lq // Q_BLOCK
    kf = k.astype(jnp.float32)
    qb = q.reshape(b, n_blk, Q_BLOCK, N_KV_HEADS, Q_PER_KV, HEAD_DIM).transpose(1, 0, 2, 3, 4, 5)
    scale = HEAD_DIM ** -0.5

    def one_block(q_blk):
        s = jnp.einsum('bqkgd,bskd->bkgqs', q_blk.astype(jnp.float32), kf) * scale
        p = jax.nn.softmax(s, axis=-1).astype(v.dtype)
        return jnp.einsum('bkgqs,bskd->bqkgd', p, v)

    o = lax.map(one_block, qb)
    return o.transpose(1, 0, 2, 3, 4, 5).reshape(b, lq, ATTN_WIDTH)

def fourier_mix(u):
    b, l = u.shape[0], u.shape[1]
    ug = u.reshape(b, l, N_FOURIER_GROUPS, FOURIER_GROUP_DIM).astype(jnp.float32)
    z = jnp.fft.fft2(ug, axes=(1, 3), norm='ortho')
    return jnp.real(z).reshape(b, l, FOURIER_WIDTH).astype(u.dtype)

def parallel_fourier_gqa(h_lat, h_ctx, w_in, q_gain, k_gain, w_out, ang_row, ang_col, ctx_out):
    q, k, v, f = jnp.split(h_lat @ w_in, EVEN_SPLITS, axis=-1)
    q = rope_2d(rmsnorm(heads(q, N_Q_HEADS), q_gain), ang_row, ang_col)
    k = rope_2d(rmsnorm(heads(k, N_KV_HEADS), k_gain), ang_row, ang_col)
    v = heads(v, N_KV_HEADS)
    if ctx_out:
        q_c, k_c, v_c, f_c = jnp.split(h_ctx @ w_in, EVEN_SPLITS, axis=-1)
        q_c = rmsnorm(heads(q_c, N_Q_HEADS), q_gain)
    else:
        k_c, v_c = jnp.split(h_ctx @ w_in[:, ATTN_WIDTH:ATTN_WIDTH + 2 * KV_WIDTH], 2, axis=-1)
    k_c = rmsnorm(heads(k_c, N_KV_HEADS), k_gain)
    v_c = heads(v_c, N_KV_HEADS)
    attn = gqa_attend(q, jnp.concatenate([k, k_c], axis=1), jnp.concatenate([v, v_c], axis=1))
    y_lat = jnp.concatenate([attn, fourier_mix(f)], axis=-1) @ w_out
    y_ctx = None
    if ctx_out:
        attn_c = gqa_attend(q_c, k_c, v_c)
        y_ctx = jnp.concatenate([attn_c, fourier_mix(f_c)], axis=-1) @ w_out
    return y_lat, y_ctx

def short_conv3(u, w):
    up = jnp.pad(u, ((0, 0), (1, 1), (0, 0)))
    return up[:, :-2] * w[0] + up[:, 1:-1] * w[1] + up[:, 2:] * w[2]

def gated_short_conv(h, w_in, conv_w, w_out):
    b_gate, c_gate, u = jnp.split(h @ w_in, 3, axis=-1)
    return (b_gate * short_conv3(c_gate * u, conv_w)) @ w_out

def swiglu(h, w_gate, w_up, w_down):
    return (jax.nn.silu(h @ w_gate) * (h @ w_up)) @ w_down

def moe_swiglu(h, router, w_gate, w_up, w_down):
    logits = (h @ router).astype(jnp.float32)
    probs = jax.nn.softmax(logits, axis=-1)
    vals, idx = lax.top_k(probs, TOP_K)
    wts = vals / jnp.sum(vals, axis=-1, keepdims=True)
    combine = jnp.sum(jax.nn.one_hot(idx, N_EXPERTS, dtype=jnp.float32) * wts[..., None], axis=-2)
    combine = combine.astype(h.dtype)
    out = jnp.zeros_like(h)
    for e in range(N_EXPERTS):
        out = out + combine[..., e:e + 1] * swiglu(h, w_gate[e], w_up[e], w_down[e])
    return out

def _normal(key, shape, fan_in):
    return jax.random.normal(key, shape, jnp.float32) * (fan_in ** -0.5)

def setup_inputs(seed: int = 0) -> dict:
    key = jax.random.key(seed)
    ks = jax.random.split(key, 21)
    D = D_MODEL
    f32 = jnp.float32
    return {
        'x': jax.random.normal(ks[0], (BATCH, SEQ, D), f32),
        'c': jax.random.normal(ks[1], (BATCH, D), f32),
        'ctx': jax.random.normal(ks[2], (BATCH, CTX_LEN, D), f32),
        'c_ctx': jax.random.normal(ks[3], (D,), f32),
        'ada_w': _normal(ks[4], (DEPTH, D, 6 * D), D),
        'ada_b': 0.02 * jax.random.normal(ks[5], (DEPTH, 6 * D), f32),
        'norm_w': 1.0 + 0.05 * jax.random.normal(ks[6], (DEPTH, 4, D), f32),
        'e_w_in': _normal(ks[7], (N_EVEN, D, EVEN_IN_WIDTH), D),
        'e_q_gain': 1.0 + 0.05 * jax.random.normal(ks[8], (N_EVEN, HEAD_DIM), f32),
        'e_k_gain': 1.0 + 0.05 * jax.random.normal(ks[9], (N_EVEN, HEAD_DIM), f32),
        'e_w_out': _normal(ks[10], (N_EVEN, MIX_WIDTH, D), MIX_WIDTH),
        'e_ffn_gate': _normal(ks[11], (N_EVEN, D, D_FF), D),
        'e_ffn_up': _normal(ks[12], (N_EVEN, D, D_FF), D),
        'e_ffn_down': _normal(ks[13], (N_EVEN, D_FF, D), D_FF),
        'o_w_in': _normal(ks[14], (N_ODD, D, 3 * CONV_WIDTH), D),
        'o_conv_w': _normal(ks[15], (N_ODD, CONV_K, CONV_WIDTH), CONV_K),
        'o_w_out': _normal(ks[16], (N_ODD, CONV_WIDTH, D), CONV_WIDTH),
        'o_router': _normal(ks[17], (N_ODD, D, N_EXPERTS), D),
        'o_exp_gate': _normal(ks[18], (N_ODD, N_EXPERTS, D, D_EXPERT), D),
        'o_exp_up': _normal(ks[19], (N_ODD, N_EXPERTS, D, D_EXPERT), D),
        'o_exp_down': _normal(ks[20], (N_ODD, N_EXPERTS, D_EXPERT, D), D_EXPERT),
    }

def reference(x, c, ctx, c_ctx, ada_w, ada_b, norm_w, e_w_in, e_q_gain, e_k_gain, e_w_out,
              e_ffn_gate, e_ffn_up, e_ffn_down, o_w_in, o_conv_w, o_w_out, o_router,
              o_exp_gate, o_exp_up, o_exp_down):
    ang_row, ang_col = axial_rope_angles(x.shape[1])
    s_c = jax.nn.silu(c)
    s_ctx = jax.nn.silu(c_ctx)
    for i in range(DEPTH):
        even = (i % 2 == 0)
        ctx_out = any(j % 2 == 0 for j in range(i + 1, DEPTH))
        ctx_in = even or ctx_out
        g_pre_mix, g_post_mix, g_pre_ch, g_post_ch = norm_w[i, 0], norm_w[i, 1], norm_w[i, 2], norm_w[i, 3]
        sh1, sc1, gt1, sh2, sc2, gt2 = jnp.split((s_c @ ada_w[i] + ada_b[i])[:, None, :], 6, axis=-1)
        h_lat = modulate(x, g_pre_mix, sh1, sc1)
        h_ctx = None
        if ctx_in:
            csh1, csc1, cgt1, csh2, csc2, cgt2 = jnp.split(s_ctx @ ada_w[i] + ada_b[i], 6, axis=-1)
            h_ctx = modulate(ctx, g_pre_mix, csh1, csc1)
        if even:
            e = i // 2
            y_lat, y_ctx = parallel_fourier_gqa(h_lat, h_ctx, e_w_in[e], e_q_gain[e], e_k_gain[e],
                                                e_w_out[e], ang_row, ang_col, ctx_out)
        else:
            o = i // 2
            y_lat = gated_short_conv(h_lat, o_w_in[o], o_conv_w[o], o_w_out[o])
            y_ctx = gated_short_conv(h_ctx, o_w_in[o], o_conv_w[o], o_w_out[o]) if ctx_out else None
        x = x + gt1 * rmsnorm(y_lat, g_post_mix)
        if ctx_out:
            ctx = ctx + cgt1 * rmsnorm(y_ctx, g_post_mix)
        h_lat = modulate(x, g_pre_ch, sh2, sc2)
        if even:
            y_lat = swiglu(h_lat, e_ffn_gate[e], e_ffn_up[e], e_ffn_down[e])
        else:
            y_lat = moe_swiglu(h_lat, o_router[o], o_exp_gate[o], o_exp_up[o], o_exp_down[o])
        x = x + gt2 * rmsnorm(y_lat, g_post_ch)
        if ctx_out:
            h_ctx = modulate(ctx, g_pre_ch, csh2, csc2)
            if even:
                y_ctx = swiglu(h_ctx, e_ffn_gate[e], e_ffn_up[e], e_ffn_down[e])
            else:
                y_ctx = moe_swiglu(h_ctx, o_router[o], o_exp_gate[o], o_exp_up[o], o_exp_down[o])
            ctx = ctx + cgt2 * rmsnorm(y_ctx, g_post_ch)
    return x


_drawn_inputs = setup_inputs


def setup_inputs(seed=0):
    import zlib

    import numpy as np

    out = dict(_drawn_inputs(seed))
    spreads = {}
    factors = {'e_q_gain': 3.7, 'e_k_gain': 2.891}
    for name, (base, spread) in spreads.items():
        noise = np.random.default_rng([zlib.crc32(name.encode()), seed]).standard_normal(out[name].shape)
        drawn = base * np.exp(spread * noise) if base else spread * noise
        out[name] = jnp.asarray(drawn.astype(out[name].dtype))
    for name, factor in factors.items():
        out[name] = (out[name] * factor).astype(out[name].dtype)
    return out
```

```python
from contextlib import ExitStack

import numpy as np

import concourse.bass as bass
from concourse import mybir

P = 128
D = 1024
KD = D // P
SEQ = 256
TB = SEQ // P
CTX = 256
NKB = (SEQ + CTX) // P
HD = 64
NQ, NKV = 12, 4
PAIRS = NQ // 2
AW, KW, FW = NQ * HD, NKV * HD, 256
FG = 64
GRID_W = 64
D_FF = 2816
NF = D_FF // P
E = 8
DE = 3584
NFE = DE // P
EPS = 1e-6
SCALE = HD ** -0.5
RING = 7
UNIT = 4096
BANK = 512
WIDTHS = (64, 96, 128, 160, 256)
HEAD_ORDER = [h for g in range(2) for i in range(3) for h in (6 * g + i, 6 * g + 3 + i)]

F32 = mybir.dt.float32
I32 = mybir.dt.int32
ALU = mybir.AluOpType
ACT = mybir.ActivationFunctionType
AX = mybir.AxisListType.X


def stream_order():
    order = [("mod", j) for j in range(4)] + [("win", j) for j in range(3)]
    order += [("ada0", s, h) for s in range(4) for h in range(2)]
    order += [("wout", j) for j in range(2)]
    ada1 = [("ada1", s, h) for s in range(6) for h in range(2)]
    for u in range(NF // 2):
        order.append(("gu", u))
        order += ada1[:2] if u == 0 else ada1[u + 1:u + 2]
    order += [("down", j) for j in range(-(-NF // 4))]
    order += [("owin", j) for j in range(6)] + [("owout", j) for j in range(2)]
    return order


ORDER = stream_order()
AT = {what: n for n, what in enumerate(ORDER)}
BASE = len(ORDER)
GU_UNITS = NFE // 2
PER_EXPERT = GU_UNITS + NFE // 4
UNITS = BASE + E * PER_EXPERT
assert PER_EXPERT % RING == 0
LAPS = PER_EXPERT // RING

V_C, V_B0, V_G, V_CONV, V_ROUTER, V_END = 0, 16, 32, 64, 88, 152
C_ID, C_ONE, C_REV, C_END = 0, 128, 256, 264


def build(nc, stream, x_in, ctx_in, vecs, consts, rope, dft, gains, ada_b, norm_w, late, out):
    ctx = ExitStack()
    with ctx:
        def sb(name, shape, dt=F32):
            return ctx.enter_context(nc.sbuf_tensor(name, shape, dt))

        def sem(name):
            return ctx.enter_context(nc.semaphore(name))

        ring = sb("ring", [P, RING, UNIT])
        x = sb("x", [P, TB, D])
        hT = sb("hT", [P, KD, SEQ])
        xn = sb("xn", [P, TB, D])
        aT = sb("aT", [P, NFE * SEQ])
        hTe = sb("hTe", [P, KD, SEQ])
        acc = sb("acc", [P, 6 * D])
        gg = sb("gg", [P, 2, D])
        vec = sb("vec", [P, V_END])
        cst = sb("cst", [P, C_END])
        silu_c = sb("silu_c", [P, KD, 2])
        ab = sb("ab", [P, 5, 2, KD])
        mods0 = sb("mods0", [P, 2, KD, 2])
        stat = sb("stat", [P, 128])
        eps = sb("eps", [P, 1])
        width_at = sb("width_at", [1, E + 1], I32)
        ps = ctx.enter_context(nc.psum_tensor("ps", [P, 8, BANK], F32))

        ident, ones, rev = cst[:, C_ID:C_ID + P], cst[:, C_ONE:C_ONE + P], cst[:, C_REV:C_REV + E]
        ctx_x = hTe[:, :, :].rearrange("p k t -> p (k t)").rearrange("p (b d) -> p b d", b=TB)
        hTc = acc[:, 4096:6144].rearrange("p (k t) -> p k t", k=KD)
        kT = acc[:, 4096:5120].rearrange("p (j t) -> p j t", j=2)
        fA = acc[:, 5120:6144].rearrange("p (j n) -> p j n", j=2)
        qT = hTe[:, 0:PAIRS, :]
        mixT = hT
        at_o = xn[:, :, :].rearrange("p b d -> p (b d)")[:, 0:TB * AW].rearrange("p (b n) -> p b n", b=TB)
        q_tok = aT[:, 0:1536].rearrange("p (b n) -> p b n", b=TB)
        k_tok = aT[:, 1536:2560].rearrange("p (b n) -> p b n", b=NKB)
        probs = aT[:, 0:1536].rearrange("p (r n) -> p r n", r=3)
        probsT = aT[:, 1536:2560].rearrange("p (r n) -> p r n", r=2)
        v_tok = aT[:, 2560:3584].rearrange("p (b n) -> p b n", b=NKB)
        f_tok = aT[:, 3584:4096].rearrange("p (b n) -> p b n", b=TB)
        dftL = aT[:, 4096:5120].rearrange("p (b n) -> p b n", b=TB)
        dftD = aT[:, 5120:5376].rearrange("p (b n) -> p b n", b=2)
        roped = aT[:, 5376:5888]
        rope_t = aT[:, 5888:6400].rearrange("p (w c b n) -> p w c b n", w=2, c=2, b=TB)
        gain_t = aT[:, 6400:6656].rearrange("p (w c n) -> p w c n", w=2, c=2)
        rotated = aT[:, 6656:7168]
        gated = hTe[:, 0:4, :]
        gated_e = hT[:, 0:4, :]
        conv_in = hTe[:, :, :].rearrange("p k t -> p (k t)")[:, 0:2 * (SEQ + 2)].rearrange("p (r n) -> p r n", r=2)
        conv_c = hTe[:, 4:6, :]
        conv_s = hTe[:, 6:8, :]
        y_sum = acc[:, 0:2048].rearrange("p (b d) -> p b d", b=TB)
        y_slot = acc[:, 2048:4096].rearrange("p (b d) -> p b d", b=2)
        sel = acc[:, 4096:4608].rearrange("p (b s) -> p b s", b=TB)
        selw = acc[:, 4608:5120].rearrange("p (b s) -> p b s", b=TB)
        selT = acc[:, 5120:5632].rearrange("p (b t) -> p b t", b=2)
        iota, before = acc[:, 5632:5888], acc[:, 5888:6016]

        def small(a, n, w):
            return acc[:, 6016 + a:6016 + a + 2 * n].rearrange("p (b e) -> p b e", b=TB)[:, :, 0:w]

        logit, tmp8, first, second, chosen = (small(16 * i, 8, 8) for i in range(5))
        slot_of, weight_of = small(80, 9, 9), small(98, 9, 9)

        landed = [sem(f"landed{s}") for s in range(RING)]
        used = [sem(f"used{s}") for s in range(RING)]
        small_in, x_in_s, ctx_in_s, tables_in = sem("small_in"), sem("x_in"), sem("ctx_in"), sem("tables_in")
        rows_in, bias_in, late_in = sem("rows_in"), sem("bias_in"), sem("late_in")
        acc_zero, tables_ok, psum_zero, eps_ok = sem("acc_zero"), sem("tables_ok"), sem("psum_zero"), sem("eps_ok")
        silu_ok, mod_sums, mod_ok = sem("silu_ok"), sem("mod_sums"), sem("mod_ok")
        dchain, achain, pchain = sem("dve_chain"), sem("act_chain"), sem("pool_chain")
        root, xn_ok, xT_ok, x_ok = sem("root"), sem("xn_ok"), sem("xT_ok"), sem("x_ok")
        hT_act, hT_dve, raw_act, raw_dve = sem("hT_act"), sem("hT_dve"), sem("raw_act"), sem("raw_dve")
        proj, square, ssum, qk_root = sem("proj"), sem("square"), sem("ssum"), sem("qk_root")
        head_ok, v_ok = sem("head_ok"), sem("v_ok")
        kT_ps, kT_ok, fA_ps, fA_ok, qT_ps, qT_ok, f_ps, f_ok = (
            sem(n) for n in ("kT_ps", "kT_ok", "fA_ps", "fA_ok", "qT_ps", "qT_ok", "f_ps", "f_ok"))
        score, negmax, prob, probT_ps, probT_ok, pv, o_ok = (
            sem(n) for n in ("score", "negmax", "prob", "probT_ps", "probT_ok", "pv", "o_ok"))
        oT_ps, oT_ok, y_ps = sem("oT_ps"), sem("oT_ok"), sem("y_ps")
        red_ps, red_ok, ada_acc = sem("red_ps"), sem("red_ok"), sem("ada_acc")
        gu_ps, silu_out, a_ok = sem("gu_ps"), sem("silu_out"), sem("a_ok")
        c_out, z_ok, conv_ps = sem("c_out"), sem("z_ok"), sem("conv_ps")
        logit_ps, exp_in, exp_out, chosen_ok, rank_ps, width_ok = (
            sem(n) for n in ("logit_ps", "exp_in", "exp_out", "chosen_ok", "rank_ps", "width_ok"))
        sel_ok, selw_ok, gather_ps, hTe_act, hTe_dve = (
            sem(n) for n in ("sel_ok", "selw_ok", "gather_ps", "hTe_act", "hTe_dve"))
        e_ps, e_silu, e_a, selT_ps, selT_ok, ye_ps, ye_act, ye_dve, comb_ps, comb_ok = (
            sem(n) for n in ("e_ps", "e_silu", "e_a", "selT_ps", "selT_ok", "ye_ps", "ye_act", "ye_dve",
                             "comb_ps", "comb_ok"))
        stored = sem("stored")

        def slot(what):
            return ring[:, AT[what] % RING, :]

        def wait_landed(eng, what):
            n = AT[what]
            eng.wait_ge(landed[n % RING], 16 * (n // RING + 1))

        def used_up(ins, what):
            ins.then_inc(used[AT[what] % RING], 1)

        def pre_stat(norm, b):
            c = 4 * (TB * norm + b)
            return stat[:, c:c + 1], stat[:, c + 1:c + 2], stat[:, c + 2:c + 3]

        def post_stat(norm, b):
            c = 40 + 3 * (TB * norm + b)
            return stat[:, c:c + 1], stat[:, c + 1:c + 2], stat[:, c + 2:c + 3]

        HEADS = [4, 4, 4, 4, 8, 8, 4, 4]
        hstat = sb("hstat", [P, 3, 40])
        att = sb("att", [P, 4, TB * NQ])
        rt = sb("rt", [P, 8, TB])

        def hcols(i, blk):
            c = sum(HEADS[:blk])
            return hstat[:, i, c:c + HEADS[blk]]

        def y_bank(b):
            return ps[:, 4 + 2 * b:6 + 2 * b, :]

        block = ctx.enter_context(nc.Block())

        @block.sync
        def _(sp):
            for s in range(RING):
                sp.dma_start(ring[:, s, :], stream[s, :, :]).then_inc(landed[s], 16)
            with sp.Fori(1, UNITS // RING) as lap:
                for s in range(RING):
                    sp.wait_ge(used[s], lap)
                    sp.dma_start(ring[:, s, :], stream[lap * RING + s, :, :]).then_inc(landed[s], 16)
            for s in range(UNITS % RING):
                sp.wait_ge(used[s], UNITS // RING)
                sp.dma_start(ring[:, s, :], stream[UNITS - UNITS % RING + s, :, :]).then_inc(landed[s], 16)

        @block.gpsimd
        def _(pool):
            pool.memset(acc[:, 0:4096], 0.0).then_inc(pchain, 1)
            pool.dma_start(dftL, dft[:, 0:1024].rearrange("p (b n) -> p b n", b=TB)).then_inc(tables_in, 16)
            pool.dma_start(dftD, dft[:, 1024:1280].rearrange("p (b n) -> p b n", b=2)).then_inc(tables_in, 16)
            for w in range(2):
                pool.dma_start(rope_t[:, w, :, :, :].rearrange("p c b n -> p (c b n)"), rope).then_inc(tables_in, 16)
            pool.dma_start(gain_t.rearrange("p w c n -> p (w c n)"), gains.to_broadcast([P, 256])).then_inc(tables_in, 16)
            pool.wait_ge(pchain, 1)
            pool.dma_start(acc[0:1, 0:4096], ada_b[0:1, 2048:6144]).then_inc(bias_in, 16)
            for i in range(2):
                pool.dma_start(gg[:, i, :], norm_w[2 * i + 1:2 * i + 2, :].to_broadcast([P, D])).then_inc(rows_in, 16)
            pool.wait_ge(red_ps, 5)
            pool.wait_ge(score, TB * NQ)
            pool.wait_ge(f_ps, 1)
            pool.memset(acc[:, :], 0.0).then_inc(pchain, 1)
            pool.wait_ge(pchain, 2)
            pool.dma_start(acc[0:1, :], ada_b[1:2, :]).then_inc(bias_in, 16)
            pool.wait_ge(x_ok, 2 * TB)
            for i in range(2):
                pool.dma_start(gg[:, i, :], norm_w[4 + 2 * i + 1:4 + 2 * i + 2, :].to_broadcast([P, D])).then_inc(rows_in, 16)
            pool.wait_ge(red_ps, 10)
            pool.dma_start(acc[:, 5632:6016], late).then_inc(late_in, 16)

        @block.scalar
        def _(act):
            links = [0]

            def link(ins):
                links[0] += 1
                ins.then_inc(achain, 1)
                act.wait_ge(achain, links[0])

            def rms(src, junk, st, n):
                link(act.activation(junk, src, ACT.Square, accum_out=st[0]))
                act.activation(st[1], st[0], ACT.Sqrt, bias=eps[:, 0:1], scale=1.0 / n).then_inc(root, 1)

            act.dma_start(vec[:, :], vecs).then_inc(small_in, 16)
            act.dma_start(cst[:, :], consts).then_inc(small_in, 16)
            act.dma_start(x[:, :, :], x_in.rearrange("(b p) d -> p b d", p=P)).then_inc(x_in_s, 16)
            act.dma_start(ctx_x, ctx_in.rearrange("(b p) d -> p b d", p=P)).then_inc(ctx_in_s, 16)
            act.wait_ge(small_in, 32)
            act.activation(silu_c[:, :, :], vec[:, V_C:V_C + 2 * KD].rearrange("p (k v) -> p k v", v=2),
                           ACT.Silu).then_inc(silu_ok, 1)
            act.wait_ge(eps_ok, 1)
            act.wait_ge(x_in_s, 16)
            for b in range(TB):
                rms(x[:, b, :], xn[:, b, :], pre_stat(0, b), D)
            act.wait_ge(ctx_in_s, 16)
            for b in range(TB):
                rms(ctx_x[:, b, :], acc[:, 4096 + D * b:4096 + D * (b + 1)], pre_stat(1, b), D)
            act.wait_ge(xT_ok, TB)
            for j in range(4):
                act.activation(hT[:, 2 * j:2 * j + 2, :].rearrange("p k t -> p (k t)"), ps[:, j, :],
                               ACT.Copy).then_inc(raw_act, 1)
            act.wait_ge(mod_ok, 1)
            act.wait_ge(raw_dve, 4)
            for k in range(KD):
                act.activation(hTc[:, k, :], hTc[:, k, :], ACT.Identity, bias=ab[:, 1, 1, k:k + 1],
                               scale=ab[:, 1, 0, k:k + 1]).then_inc(hT_act, 1)
            for blk in range(8):
                nh = HEADS[blk]
                act.wait_ge(proj, blk + 1)
                if blk < NKB:
                    dst = k_tok[:, blk, :]
                else:
                    dst = q_tok[:, blk % 2, (0 if blk < 6 else 512):(512 if blk < 6 else 768)]
                act.activation(dst, ps[:, blk, 0:nh * HD], ACT.Square).then_inc(square, 1)
                if blk < NKB:
                    act.activation(v_tok[:, blk, :], ps[:, blk, 256:512], ACT.Copy).then_inc(v_ok, 1)
                elif blk >= 6:
                    act.activation(f_tok[:, blk % 2, :], ps[:, blk, 256:512], ACT.Copy).then_inc(v_ok, 1)
                act.wait_ge(ssum, blk + 1)
                act.activation(hcols(1, blk), hcols(0, blk), ACT.Sqrt, bias=eps[:, 0:1],
                               scale=1.0 / HD).then_inc(qk_root, 1)
            act.wait_ge(kT_ps, 2)
            for j in range(2):
                act.activation(kT[:, j, :], ps[:, j, :], ACT.Copy).then_inc(kT_ok, 1)
            act.wait_ge(qT_ps, 1)
            for j in range(3):
                act.activation(qT[:, 2 * j:2 * j + 2, :].rearrange("p k t -> p (k t)"), ps[:, 4 + j, :],
                               ACT.Copy).then_inc(qT_ok, 1)
            act.wait_ge(f_ps, 1)
            act.activation(mixT[:, 6:8, :].rearrange("p k t -> p (k t)"), ps[:, 7, :], ACT.Copy).then_inc(f_ok, 1)
            for n in range(TB * NQ + 2):
                if n < TB * NQ:
                    act.wait_ge(negmax, n + 1)
                    if n >= 3:
                        act.wait_ge(probT_ps, n - 2)
                    act.activation(probs[:, n % 3, :], ps[:, n % 3, :], ACT.Exp, bias=att[:, 1, n:n + 1],
                                   scale=SCALE, accum_out=att[:, 2, n:n + 1]).then_inc(prob, 1)
                m = n - 2
                if m >= 0:
                    act.wait_ge(probT_ps, m + 1)
                    if m >= 2:
                        act.wait_ge(pv, m - 1)
                    act.activation(probsT[:, m % 2, :], ps[:, 3 + m % 2, :], ACT.Copy).then_inc(probT_ok, 1)
            act.wait_ge(oT_ps, 1)
            for j in range(3):
                act.activation(mixT[:, 2 * j:2 * j + 2, :].rearrange("p k t -> p (k t)"), ps[:, j, :],
                               ACT.Copy).then_inc(oT_ok, 1)

            def post_pre(post, pre):
                for b in range(TB):
                    act.wait_ge(y_ps, TB * post + b + 1)
                    rms(y_bank(b).rearrange("p a n -> p (a n)"), xn[:, b, :], post_stat(post, b), D)
                    act.wait_ge(x_ok, TB * post + b + 1)
                    rms(x[:, b, :], xn[:, b, :], pre_stat(pre, b), D)
                act.wait_ge(xT_ok, TB * (pre + 1))
                for k in range(KD // 2):
                    act.activation(hT[:, k, :], ps[:, k // 2, (k % 2) * SEQ:(k % 2 + 1) * SEQ], ACT.Identity, bias=ab[:, pre, 1, k:k + 1],
                                   scale=ab[:, pre, 0, k:k + 1]).then_inc(hT_act, 1)

            post_pre(0, 2)
            for j in range(NF):
                act.wait_ge(gu_ps, j + 1)
                act.activation(gated[:, j % 4, :], ps[:, j % 4, 0:SEQ], ACT.Silu).then_inc(silu_out, 1)
            post_pre(1, 3)
            for j in range(KD):
                act.wait_ge(conv_ps, j + 1)
                if j >= 2:
                    act.wait_ge(z_ok, j - 1)
                act.activation(conv_c[:, j % 2, :], ps[:, 2 * (j % 2), SEQ:2 * SEQ], ACT.Copy).then_inc(c_out, 1)
            post_pre(2, 4)
            act.wait_ge(exp_in, 1)
            act.activation(rt[:, 4, :], rt[:, 3, :], ACT.Exp).then_inc(exp_out, 1)

            def take_gather(count):
                for k in range(KD // 2):
                    if k % 2 == 0:
                        act.wait_ge(gather_ps, count + k // 2 + 1)
                    act.activation(hTe[:, k, :], ps[:, k // 2, (k % 2) * SEQ:(k % 2 + 1) * SEQ], ACT.Identity,
                                   bias=ab[:, 4, 1, k:k + 1], scale=ab[:, 4, 0, k:k + 1]).then_inc(hTe_act, 1)

            take_gather(0)
            with act.Fori(0, E) as e:
                for j in range(NFE):
                    act.wait_ge(e_ps, e * NFE + j + 1)
                    act.activation(gated_e[:, j % 4, :], ps[:, j % 4, 0:SEQ], ACT.Silu).then_inc(e_silu, 1)
                act.wait_ge(selT_ps, e + 1)
                act.activation(selT[:, :, :].rearrange("p b t -> p (b t)"), ps[:, 4, :], ACT.Copy).then_inc(selT_ok, 1)
                act.wait_ge(ye_ps, e + 1)
                for b in range(2):
                    act.activation(y_slot[:, b, 0:BANK], ps[:, 6 - 2 * b, :], ACT.Copy).then_inc(ye_act, 1)
                take_gather(e * 4 + 4)
            for b in range(TB):
                act.wait_ge(comb_ok, 4 * E + 2 * b + 2)
                rms(y_sum[:, b, :], xn[:, b, :], post_stat(3, b), D)
            for b in range(TB):
                act.wait_ge(x_ok, 3 * TB + b + 1)
                act.dma_start(out[b * P:(b + 1) * P, :], x[:, b, :]).then_inc(stored, 16)
            act.wait_ge(stored, 16 * TB)

        @block.vector
        def _(dve):
            links = [0]

            def link(ins):
                links[0] += 1
                ins.then_inc(dchain, 1)
                dve.wait_ge(dchain, links[0])

            dve.memset(eps[:, :], EPS).then_inc(eps_ok, 1)
            dve.memset(ps[:, :, :], 0.0).then_inc(psum_zero, 1)

            roots = [0]

            def norm_rows(src, dst, st):
                roots[0] += 1
                dve.wait_ge(root, roots[0])
                link(dve.reciprocal(st[2], st[1]))
                dve.tensor_scalar(dst, src, st[2], None, ALU.mult).then_inc(xn_ok, 1)

            dve.wait_ge(x_in_s, 16)
            for b in range(TB):
                norm_rows(x[:, b, :], xn[:, b, :], pre_stat(0, b))
            dve.wait_ge(ctx_in_s, 16)
            for b in range(TB):
                norm_rows(ctx_x[:, b, :], ctx_x[:, b, :], pre_stat(1, b))
            dve.wait_ge(xT_ok, 2 * TB)
            for j in range(4):
                dve.tensor_copy(hTc[:, 2 * j:2 * j + 2, :].rearrange("p k t -> p (k t)"),
                                ps[:, 4 + j, :]).then_inc(raw_dve, 1)
            dve.wait_ge(tables_in, 80)
            for w in range(2):
                for c in range(2):
                    last = dve.tensor_tensor(rope_t[:, w, c, :, :], rope_t[:, w, c, :, :],
                                             gain_t[:, w, c:c + 1, :].to_broadcast([P, TB, HD]), ALU.mult)
            link(last)
            dve.wait_ge(small_in, 32)
            dve.wait_ge(mod_sums, 1)
            b0 = vec[:, V_B0:V_B0 + 16]
            link(dve.tensor_tensor(mods0[:, :, :, :].rearrange("p s k v -> p (s k) v"),
                                   ps[:, 0, 0:32].rearrange("p (m v) -> p m v", v=2),
                                   b0.unsqueeze(2).to_broadcast([P, 16, 2]), ALU.add))
            for v in range(2):
                dve.tensor_copy(ab[:, v, 1, :], mods0[:, 0, :, v])
                last = dve.scalar_tensor_tensor(out=ab[:, v, 0, :], in0=mods0[:, 1, :, v], scalar=1.0,
                                                in1=vec[:, V_G:V_G + KD], op0=ALU.add, op1=ALU.mult)
            last.then_inc(mod_ok, 1)
            dve.wait_ge(mod_ok, 1)
            dve.wait_ge(raw_act, 4)
            for k in range(KD):
                dve.tensor_scalar(hT[:, k, :], hT[:, k, :], ab[:, 0, 0, k:k + 1], ab[:, 0, 1, k:k + 1],
                                  ALU.mult, ALU.add).then_inc(hT_dve, 1)

            def ada_unit(layer, s, h):
                what = (f"ada{layer}", s, h)
                if s == 0 and h == 0:
                    dve.wait_ge(bias_in, 16 * (layer + 1))
                wait_landed(dve, what)
                dst = acc[:, s * D:(s + 1) * D]
                for k in range(4):
                    last = dve.scalar_tensor_tensor(out=dst, in0=slot(what)[:, k * D:(k + 1) * D],
                                                    scalar=silu_c[:, 4 * h + k, 0:1], in1=dst,
                                                    op0=ALU.mult, op1=ALU.add)
                    if k < 3:
                        link(last)
                used_up(last, what)
                n = AT[what]
                dve.wait_ge(used[n % RING], n // RING + 1)
                dve.sem_inc(ada_acc, 1)

            def head_block(blk):
                nh = HEADS[blk]
                w = 1 if blk < NKB else 0
                if blk < NKB:
                    dst = k_tok[:, blk, :]
                else:
                    dst = q_tok[:, blk % 2, (0 if blk < 6 else 512):(512 if blk < 6 else 768)]
                heads = dst.rearrange("p (h d) -> p h d", d=HD)
                dve.wait_ge(square, blk + 1)
                dve.tensor_reduce(hcols(0, blk), heads, AX, ALU.add).then_inc(ssum, 1)
                dve.wait_ge(qk_root, blk + 1)
                link(dve.reciprocal(hcols(2, blk), hcols(1, blk)))
                link(dve.tensor_tensor(heads, ps[:, blk, 0:nh * HD].rearrange("p (h d) -> p h d", d=HD),
                                       hcols(2, blk).unsqueeze(2).to_broadcast([P, nh, HD]), ALU.mult))
                if 2 <= blk < NKB:
                    dve.tensor_tensor(heads, heads, gain_t[:, 1, 0:1, :].to_broadcast([P, nh, HD]),
                                      ALU.mult).then_inc(head_ok, 1)
                    return
                b = blk % 2
                dve.tensor_tensor(roped[:, 0:nh * HD].rearrange("p (h d) -> p h d", d=HD), heads,
                                  rope_t[:, w, 0, b:b + 1, :].to_broadcast([P, nh, HD]), ALU.mult)
                for a in range(2):
                    part = dst.rearrange("p (h x a d) -> p h x a d", x=2, a=2, d=16)[:, :, :, 1 - a, :]
                    to = rotated[:, 0:nh * HD].rearrange("p (h x a d) -> p h x a d", x=2, a=2, d=16)[:, :, :, a, :]
                    tab = rope_t[:, w, 1, b, :].rearrange("p (x a d) -> p x a d", x=2, a=2)[:, :, a, :]
                    last = dve.tensor_tensor(to, part, tab.unsqueeze(1).to_broadcast([P, nh, 2, 16]), ALU.mult)
                link(last)
                dve.tensor_tensor(dst, roped[:, 0:nh * HD], rotated[:, 0:nh * HD], ALU.add).then_inc(head_ok, 1)
                dve.wait_ge(head_ok, blk + 1)

            for blk in range(NKB):
                head_block(blk)
            units0 = [(s, h) for s in range(4) for h in range(2)]
            for n, u in enumerate(units0):
                ada_unit(0, *u)
                if n == 0:
                    head_block(4)
                    head_block(5)
                if n == 3:
                    head_block(6)
                    head_block(7)
                    dve.wait_ge(fA_ps, 1)
                    for j in range(2):
                        dve.tensor_copy(fA[:, j, :], ps[:, 2 + j, :]).then_inc(fA_ok, 1)

            def gate_half(i):
                half = gg[:, i // 2, (i % 2) * BANK:(i % 2 + 1) * BANK]
                dve.tensor_tensor(half, half, ps[:, 7, :], ALU.mult).then_inc(red_ok, 1)

            def factors(pre, src, g):
                dve.tensor_copy(ab[:, pre, 1, :], src[:, 0:KD])
                dve.scalar_tensor_tensor(out=ab[:, pre, 0, :], in0=src[:, KD:2 * KD], scalar=1.0,
                                         in1=vec[:, V_G + KD * g:V_G + KD * (g + 1)], op0=ALU.add,
                                         op1=ALU.mult).then_inc(red_ok, 1)

            dve.wait_ge(rows_in, 32)
            for n in range(TB * NQ + 3):
                if n < TB * NQ:
                    dve.wait_ge(score, n + 1)
                    link(dve.tensor_reduce(att[:, 0, n:n + 1], ps[:, n % 3, :], AX, ALU.max))
                    dve.tensor_scalar(att[:, 1, n:n + 1], att[:, 0, n:n + 1], -SCALE, None,
                                      ALU.mult).then_inc(negmax, 1)
                m = n - 3
                if m >= 0:
                    dve.wait_ge(prob, m + 1)
                    link(dve.reciprocal(att[:, 3, m:m + 1], att[:, 2, m:m + 1]))
                    dve.wait_ge(pv, m + 1)
                    dve.tensor_scalar(at_o[:, m // NQ, (m % NQ) * HD:(m % NQ + 1) * HD], ps[:, 5 + m % 2, 0:HD],
                                      att[:, 3, m:m + 1], None, ALU.mult).then_inc(o_ok, 1)
                if 12 <= n < 22 and n % 2 == 0:
                    i = (n - 12) // 2
                    dve.wait_ge(red_ps, i + 1)
                    if i < 4:
                        gate_half(i)
                    else:
                        factors(2, ps[:, 7, 0:16], 1)

            def post_pre(post, pre):
                for b in range(TB):
                    st = post_stat(post, b)
                    roots[0] += 1
                    dve.wait_ge(root, roots[0])
                    link(dve.reciprocal(st[2], st[1]))
                    link(dve.scalar_tensor_tensor(out=xn[:, b, :], in0=y_bank(b).rearrange("p a n -> p (a n)"),
                                                  scalar=st[2], in1=gg[:, post % 2, :], op0=ALU.mult, op1=ALU.mult))
                    dve.tensor_tensor(x[:, b, :], x[:, b, :], xn[:, b, :], ALU.add).then_inc(x_ok, 1)
                    norm_rows(x[:, b, :], xn[:, b, :], pre_stat(pre, b))
                dve.wait_ge(xT_ok, TB * (pre + 1))
                for k in range(KD // 2, KD):
                    dve.tensor_scalar(hT[:, k, :], ps[:, k // 2, (k % 2) * SEQ:(k % 2 + 1) * SEQ], ab[:, pre, 0, k:k + 1],
                                      ab[:, pre, 1, k:k + 1], ALU.mult, ALU.add).then_inc(hT_dve, 1)

            post_pre(0, 2)
            units1 = [(s, h) for s in range(6) for h in range(2)]
            for j in range(NF):
                dve.wait_ge(silu_out, j + 1)
                dve.tensor_tensor(aT[:, j * SEQ:(j + 1) * SEQ], gated[:, j % 4, :], ps[:, j % 4, SEQ:2 * SEQ],
                                  ALU.mult).then_inc(a_ok, 1)
                if j % 2:
                    for _ in range(2 if j == 1 else 1):
                        ada_unit(1, *units1.pop(0))
            dve.wait_ge(red_ps, 6)
            factors(3, ps[:, 0, 0:16], 2)
            factors(4, ps[:, 0, 16:32], 3)
            post_pre(1, 3)
            link(dve.memset(conv_in, 0.0))
            for j in range(KD):
                r = j % 2
                dve.wait_ge(c_out, j + 1)
                link(dve.tensor_tensor(conv_in[:, r, 1:SEQ + 1], conv_c[:, r, :], ps[:, 2 * r + 1, 0:SEQ], ALU.mult))
                link(dve.tensor_scalar(conv_s[:, r, :], conv_in[:, r, 0:SEQ], vec[:, V_CONV + j:V_CONV + j + 1],
                                       None, ALU.mult))
                for t in (1, 2):
                    c = V_CONV + KD * t + j
                    link(dve.scalar_tensor_tensor(out=conv_s[:, r, :], in0=conv_in[:, r, t:t + SEQ],
                                                  scalar=vec[:, c:c + 1], in1=conv_s[:, r, :], op0=ALU.mult,
                                                  op1=ALU.add))
                dve.tensor_tensor(aT[:, j * SEQ:(j + 1) * SEQ], conv_s[:, r, :], ps[:, 2 * r, 0:SEQ],
                                  ALU.mult).then_inc(z_ok, 1)
            dve.wait_ge(rows_in, 64)
            for i in range(4):
                dve.wait_ge(red_ps, 7 + i)
                half = gg[:, i // 2, (i % 2) * BANK:(i % 2 + 1) * BANK]
                dve.tensor_tensor(half, half, ps[:, i, :], ALU.mult).then_inc(red_ok, 1)
            for i in range(4):
                dve.memset(y_sum[:, i // 2, (i % 2) * BANK:(i % 2 + 1) * BANK], 0.0).then_inc(comb_ok, 1)
            post_pre(2, 4)

            dve.wait_ge(late_in, 16)

            def rb(i):
                return rt[:, i, :].unsqueeze(2).to_broadcast([P, TB, E])

            revb = rev.unsqueeze(1).to_broadcast([P, TB, E])
            dve.wait_ge(logit_ps, 1)
            link(dve.tensor_copy(logit, ps[:, 4, 0:TB * E].rearrange("p (b e) -> p b e", b=TB)))

            def top(values, mask, i):
                link(dve.tensor_reduce(rt[:, i, :], values, AX, ALU.max))
                link(dve.tensor_tensor(mask, values, rb(i), ALU.is_equal))
                link(dve.tensor_tensor(mask, mask, revb, ALU.mult))
                link(dve.tensor_reduce(rt[:, 2, :], mask, AX, ALU.max))
                link(dve.tensor_tensor(mask, revb, rb(2), ALU.is_equal))

            top(logit, first, 0)
            link(dve.scalar_tensor_tensor(out=tmp8, in0=first, scalar=-3.0e38, in1=logit, op0=ALU.mult, op1=ALU.add))
            top(tmp8, second, 1)
            dve.tensor_tensor(chosen, first, second, ALU.add).then_inc(chosen_ok, 1)
            dve.tensor_tensor(rt[:, 3, :], rt[:, 1, :], rt[:, 0, :], ALU.subtract).then_inc(exp_in, 1)
            dve.wait_ge(exp_out, 1)
            link(dve.tensor_scalar(rt[:, 5, :], rt[:, 4, :], 1.0, None, ALU.add))
            link(dve.reciprocal(rt[:, 6, :], rt[:, 5, :]))
            link(dve.tensor_tensor(rt[:, 7, :], rt[:, 4, :], rt[:, 6, :], ALU.mult))
            link(dve.tensor_tensor(first, first, rb(6), ALU.mult))
            link(dve.tensor_tensor(second, second, rb(7), ALU.mult))
            link(dve.memset(weight_of, 0.0))
            link(dve.memset(slot_of, -1.0))
            link(dve.tensor_tensor(weight_of[:, :, 0:E], first, second, ALU.add))
            dve.wait_ge(rank_ps, 1)
            link(dve.scalar_tensor_tensor(out=slot_of[:, :, 0:E], in0=ps[:, 5, 0:TB * E].rearrange("p (b e) -> p b e", b=TB),
                                          scalar=1.0, in1=chosen, op0=ALU.add, op1=ALU.mult))
            link(dve.tensor_scalar(slot_of[:, :, 0:E], slot_of[:, :, 0:E], -1.0, None, ALU.add))
            count = ps[0:1, 6, 0:E]
            wsum = hstat[0:1, 0, 0:E]
            link(dve.tensor_scalar(wsum, count, float(WIDTHS[0]), None, ALU.is_gt))
            for w in WIDTHS[1:-1]:
                link(dve.scalar_tensor_tensor(out=wsum, in0=count, scalar=float(w), in1=wsum, op0=ALU.is_gt, op1=ALU.add))
            link(dve.memset(width_at[:, :], 0))
            dve.tensor_copy(width_at[0:1, 0:E], wsum).then_inc(width_ok, 1)

            def select(e, weighted):
                for b in range(TB):
                    at = slot_of[:, b, bass.ds(e, 1)]
                    if weighted:
                        last = dve.tensor_scalar(selw[:, b, :], iota, at, weight_of[:, b, bass.ds(e, 1)],
                                                 ALU.is_equal, ALU.mult)
                    else:
                        last = dve.tensor_scalar(sel[:, b, :], iota, at, None, ALU.is_equal)
                last.then_inc(selw_ok if weighted else sel_ok, 1)

            def take_gather(count):
                for k in range(KD // 2, KD):
                    if k % 2 == 0:
                        dve.wait_ge(gather_ps, count + k // 2 + 1)
                    dve.tensor_scalar(hTe[:, k, :], ps[:, k // 2, (k % 2) * SEQ:(k % 2 + 1) * SEQ],
                                      ab[:, 4, 0, k:k + 1], ab[:, 4, 1, k:k + 1], ALU.mult,
                                      ALU.add).then_inc(hTe_dve, 1)

            select(0, False)
            select(0, True)
            take_gather(0)
            with dve.Fori(0, E) as e:
                dve.wait_ge(gather_ps, e * 4 + 4)
                select(e + 1, False)
                for j in range(NFE):
                    dve.wait_ge(e_silu, e * NFE + j + 1)
                    dve.tensor_tensor(aT[:, j * SEQ:(j + 1) * SEQ], gated_e[:, j % 4, :], ps[:, j % 4, SEQ:2 * SEQ],
                                      ALU.mult).then_inc(e_a, 1)
                dve.wait_ge(selT_ps, e + 1)
                select(e + 1, True)
                dve.wait_ge(ye_ps, e + 1)
                for b in range(2):
                    dve.tensor_copy(y_slot[:, b, BANK:2 * BANK], ps[:, 7 - 2 * b, :]).then_inc(ye_dve, 1)
                take_gather(e * 4 + 4)
                for i in range(4):
                    dve.wait_ge(comb_ps, e * 4 + i + 1)
                    part = y_sum[:, i // 2, (i % 2) * BANK:(i % 2 + 1) * BANK]
                    dve.tensor_tensor(part, part, ps[:, 4 + i, :], ALU.add).then_inc(comb_ok, 1)
            for b in range(TB):
                st = post_stat(3, b)
                roots[0] += 1
                dve.wait_ge(root, roots[0])
                link(dve.reciprocal(st[2], st[1]))
                link(dve.scalar_tensor_tensor(out=xn[:, b, :], in0=y_sum[:, b, :], scalar=st[2],
                                              in1=gg[:, 1, :], op0=ALU.mult, op1=ALU.mult))
                dve.tensor_tensor(x[:, b, :], x[:, b, :], xn[:, b, :], ALU.add).then_inc(x_ok, 1)

        @block.tensor
        def _(pe):
            def turn_rows(src, bank0, order, before=None):
                for b in range(TB):
                    pe.wait_ge(xn_ok, order * TB + b + 1)
                    for k in range(KD):
                        if b == 0 and k == 1 and before:
                            used_up(last, before)
                        last = pe.transpose(ps[:, bank0 + k // 2, (k % 2) * SEQ + b * P:(k % 2) * SEQ + (b + 1) * P],
                                            src[:, b, k * P:(k + 1) * P], ident)
                    last.then_inc(xT_ok, 1)

            pe.wait_ge(small_in, 32)
            pe.wait_ge(psum_zero, 1)
            turn_rows(xn, 0, 0)
            turn_rows(ctx_x, 4, 1)
            pe.wait_ge(silu_ok, 1)
            pe.wait_ge(raw_act, 1)
            for j in range(4):
                wait_landed(pe, ("mod", j))
                w = slot(("mod", j)).rearrange("p (k n) -> p k n", k=KD)
                for m in range(4):
                    for k in range(KD):
                        c = 2 * (4 * j + m)
                        last = pe.matmul(ps[:, 0, c:c + 2], w[:, k, m * P:(m + 1) * P], silu_c[:, k, :],
                                         start=(k == 0), stop=(k == KD - 1))
                if j < 3:
                    used_up(last, ("mod", j))
            last.then_inc(mod_sums, 1)
            for blk in range(8):
                unit = ("win", 0 if blk < 4 else 1 if blk < 6 else 2)
                lhs = hTc if blk in (2, 3) else hT
                b = blk % 2
                wait_landed(pe, unit)
                w = slot(unit).rearrange("p (k n) -> p k n", k=KD)
                if blk == 0:
                    pe.wait_ge(mod_ok, 1)
                if blk == 1:
                    pe.wait_ge(raw_act, 2)
                if blk == 2:
                    pe.wait_ge(raw_act, 4)
                if blk == 4:
                    pe.wait_ge(raw_dve, 4)
                for k in range(KD):
                    if blk == 0:
                        pe.wait_ge(hT_dve, k + 1)
                    if blk == 2:
                        pe.wait_ge(hT_act, k + 1)
                    last = pe.matmul(ps[:, blk, :], lhs[:, k, b * P:(b + 1) * P], w[:, k, :],
                                     start=(k == 0), stop=(k == KD - 1))
                    if k == 0 and blk in (0, 4, 6):
                        used_up(last, {0: ("mod", 3), 4: ("win", 0), 6: ("win", 1)}[blk])
                last.then_inc(proj, 1)
            pe.wait_ge(head_ok, 4)
            pe.wait_ge(v_ok, 4)
            for j in range(2):
                for b in range(NKB):
                    last = pe.transpose(ps[:, j, b * P:(b + 1) * P], k_tok[:, b, j * P:(j + 1) * P], ident)
                    if j == 0 and b == 0:
                        used_up(last, ("win", 2))
                last.then_inc(kT_ps, 1)
            pe.wait_ge(v_ok, 6)
            pe.wait_ge(tables_in, 80)
            for j in range(2):
                for b in range(TB):
                    last = pe.matmul(ps[:, 2 + j, :], f_tok[:, b, j * P:(j + 1) * P], dftL[:, b, :],
                                     start=(b == 0), stop=(b == TB - 1))
            last.then_inc(fA_ps, 1)
            pe.wait_ge(head_ok, 8)
            for i in range(PAIRS):
                for b in range(TB):
                    last = pe.transpose(ps[:, 4 + i // 2, (i % 2) * SEQ + b * P:(i % 2) * SEQ + (b + 1) * P],
                                        q_tok[:, b, i * P:(i + 1) * P], ident)
            last.then_inc(qT_ps, 1)
            pe.wait_ge(fA_ok, 2)
            for j in range(2):
                for c in range(2):
                    last = pe.matmul(ps[:, 7, j * SEQ:(j + 1) * SEQ], dftD[:, c, :], fA[:, j, c * SEQ:(c + 1) * SEQ],
                                     start=(c == 0), stop=(c == 1))
            last.then_inc(f_ps, 1)
            pe.wait_ge(kT_ok, 2)
            pe.wait_ge(qT_ok, 3)
            pe.wait_ge(f_ok, 1)
            for n in range(TB * NQ + 3):
                if n < TB * NQ:
                    b, h = n // NQ, n % NQ
                    i, o = h // 2, HD * (h % 2)
                    if n >= 3:
                        pe.wait_ge(prob, n - 2)
                    pe.matmul(ps[:, n % 3, :], qT[o:o + HD, i, b * P:(b + 1) * P], kT[o:o + HD, i // 3, :],
                              start=True, stop=True).then_inc(score, 1)
                m = n - 2
                if 0 <= m < TB * NQ:
                    pe.wait_ge(prob, m + 1)
                    if m >= 2:
                        pe.wait_ge(probT_ok, m - 1)
                    for b in range(NKB):
                        last = pe.transpose(ps[:, 3 + m % 2, b * P:(b + 1) * P],
                                            probs[:, m % 3, b * P:(b + 1) * P], ident)
                    last.then_inc(probT_ps, 1)
                m = n - 3
                if m >= 0:
                    h = m % NQ
                    kv = 2 * (h // 6) + h % 2
                    pe.wait_ge(probT_ok, m + 1)
                    if m >= 2:
                        pe.wait_ge(o_ok, m - 1)
                    for b in range(NKB):
                        last = pe.matmul(ps[:, 5 + m % 2, 0:HD], probsT[:, m % 2, b * P:(b + 1) * P],
                                         v_tok[:, b, kv * HD:(kv + 1) * HD], start=(b == 0), stop=(b == NKB - 1))
                    last.then_inc(pv, 1)
                if 12 <= n < 22 and n % 2 == 0:
                    i = (n - 12) // 2
                    if i == 0:
                        pe.wait_ge(ada_acc, 8)
                    else:
                        pe.wait_ge(red_ok, i)
                    if i < 4:
                        c = (3 * D if i >= 2 else 0) + (i % 2) * BANK
                        last = pe.matmul(ps[:, 7, :], ones, acc[:, c:c + BANK], start=True, stop=True)
                    else:
                        for k in range(16):
                            last = pe.matmul(ps[:, 7, k:k + 1], acc[:, D + k * P:D + (k + 1) * P], ones[:, 0:1],
                                             start=True, stop=True)
                    last.then_inc(red_ps, 1)
            pe.wait_ge(o_ok, TB * NQ)
            for i in range(PAIRS):
                for b in range(TB):
                    last = pe.transpose(ps[:, i // 2, (i % 2) * SEQ + b * P:(i % 2) * SEQ + (b + 1) * P],
                                        at_o[:, b, i * P:(i + 1) * P], ident)
            last.then_inc(oT_ps, 1)

            def project(units, per_unit, nblocks, lhs, wait):
                for b in range(TB):
                    for k in range(nblocks):
                        unit = units[k // per_unit]
                        if b == 0:
                            if k % per_unit == 0:
                                wait_landed(pe, unit)
                            wait(k)
                        w = slot(unit).rearrange("p (k n) -> p k n", k=per_unit)
                        for h in range(2):
                            last = pe.matmul(ps[:, 4 + 2 * b + h, :], lhs(k)[:, b * P:(b + 1) * P],
                                             w[:, k % per_unit, h * BANK:(h + 1) * BANK],
                                             start=(k == 0), stop=(k == nblocks - 1))
                        if b == TB - 1 and (k % per_unit == per_unit - 1 or k == nblocks - 1) and k < nblocks - 1:
                            used_up(last, unit)
                    last.then_inc(y_ps, 1)

            pe.wait_ge(red_ok, 5)
            project([("wout", 0), ("wout", 1)], 4, KD, lambda k: mixT[:, k, :],
                    lambda k: pe.wait_ge(oT_ok, k // 2 + 1) if k < 6 and k % 2 == 0 else None)

            def wait_hT(pre, k):
                half = KD // 2
                pe.wait_ge(hT_act if k < half else hT_dve, KD + half * (pre - 2) + k % half + 1)

            turn_rows(xn, 0, 2, ("wout", 1))
            for u in range(NF // 2):
                wait_landed(pe, ("gu", u))
                w = slot(("gu", u)).rearrange("p (f g k n) -> p f g k n", f=2, g=2, k=KD)
                for f in range(2):
                    j = 2 * u + f
                    if j >= 4:
                        pe.wait_ge(a_ok, j - 3)
                    if j == 0:
                        for k in range(KD):
                            wait_hT(2, k)
                    for g in range(2):
                        for k in range(KD):
                            last = pe.matmul(ps[:, j % 4, g * SEQ:(g + 1) * SEQ], w[:, f, g, k, :], hT[:, k, :],
                                             start=(k == 0), stop=(k == KD - 1))
                            if u and (f, g, k) == (0, 0, 0):
                                used_up(last, ("gu", u - 1))
                    last.then_inc(gu_ps, 1)
            pe.wait_ge(ada_acc, 8 + 12)
            pe.wait_ge(a_ok, NF)
            for k in range(32):
                c = (k // 16) * 3 * D + (k % 16) * P
                last = pe.matmul(ps[:, 0, k:k + 1], acc[:, c:c + P], ones[:, 0:1], start=True, stop=True)
                if k == 0:
                    used_up(last, ("gu", NF // 2 - 1))
            last.then_inc(red_ps, 1)
            project([("down", j) for j in range(-(-NF // 4))], 4, NF, lambda k: aT[:, k * SEQ:(k + 1) * SEQ],
                    lambda k: None)
            pe.wait_ge(red_ok, 7)
            turn_rows(xn, 0, 3, ("down", -(-NF // 4) - 1))
            for i in range(3 * KD):
                unit = ("owin", i // 4)
                j, part = i // 3, i % 3
                if i % 4 == 0:
                    wait_landed(pe, unit)
                w = slot(unit).rearrange("p (f k n) -> p f k n", f=4, k=KD)
                if part == 0 and j >= 2:
                    pe.wait_ge(z_ok, j - 1)
                if i == 0:
                    for k in range(KD):
                        wait_hT(3, k)
                bank, c = (2 * (j % 2) + 1, 0) if part == 2 else (2 * (j % 2), part * SEQ)
                for k in range(KD):
                    last = pe.matmul(ps[:, bank, c:c + SEQ], w[:, i % 4, k, :], hT[:, k, :],
                                     start=(k == 0), stop=(k == KD - 1))
                    if k == 0 and i and i % 4 == 0:
                        used_up(last, ("owin", i // 4 - 1))
                if part == 2:
                    last.then_inc(conv_ps, 1)
            pe.wait_ge(z_ok, KD)
            pe.sem_inc(used[AT[("owin", 5)] % RING], 1)
            for i in range(4):
                c = (5 if i >= 2 else 2) * D + (i % 2) * BANK
                pe.matmul(ps[:, i, :], ones, acc[:, c:c + BANK], start=True, stop=True).then_inc(red_ps, 1)
            project([("owout", 0), ("owout", 1)], 4, KD, lambda k: aT[:, k * SEQ:(k + 1) * SEQ], lambda k: None)
            pe.wait_ge(red_ok, 11)
            turn_rows(xn, 0, 4, ("owout", 1))
            router = vec[:, V_ROUTER:V_ROUTER + KD * E].rearrange("p (k e) -> p k e", e=E)
            for k in range(KD):
                wait_hT(4, k)
            pe.wait_ge(x_ok, 3 * TB)
            for b in range(TB):
                for k in range(KD):
                    last = pe.matmul(ps[:, 4, b * E:(b + 1) * E], hT[:, k, b * P:(b + 1) * P], router[:, k, :],
                                     start=(k == 0), stop=(k == KD - 1))
            last.then_inc(logit_ps, 1)
            pe.wait_ge(chosen_ok, 1)
            pe.wait_ge(late_in, 16)
            pe.matmul(ps[:, 5, 0:E], before, chosen[:, 0, :], start=True, stop=True)
            pe.matmul(ps[:, 5, E:2 * E], ones, chosen[:, 0, :], start=True, stop=False)
            pe.matmul(ps[:, 5, E:2 * E], before, chosen[:, 1, :], start=False, stop=True)
            pe.matmul(ps[0:1, 6, 0:E], ones[:, 0:1], chosen[:, 0, :], start=True, stop=False)
            pe.matmul(ps[0:1, 6, 0:E], ones[:, 0:1], chosen[:, 1, :], start=False, stop=True).then_inc(rank_ps, 1)

            def width_of(at):
                return pe.value_load(width_at[0:1, bass.ds(at, 1)], min_val=0, max_val=len(WIDTHS) - 1)

            def for_width(which, body):
                for i, width in enumerate(WIDTHS):
                    with pe.If(which == i):
                        body(width)

            def gather(width, before=None):
                for j in range(4):
                    for i in range(2):
                        for b in range(TB):
                            last = pe.matmul(ps[:, j, i * SEQ:i * SEQ + width], xn[:, b, (2 * j + i) * P:(2 * j + i + 1) * P],
                                             sel[:, b, 0:width], start=(b == 0), stop=(b == TB - 1))
                            if (j, i, b) == (0, 0, 0) and before is not None:
                                last.then_inc(used[before], 1)
                    last.then_inc(gather_ps, 1)

            def landed_of(e, i):
                n = BASE + i
                pe.wait_ge(landed[n % RING], e * (16 * LAPS) + 16 * (n // RING + 1))
                return n % RING

            pe.wait_ge(width_ok, 1)
            pe.wait_ge(sel_ok, 1)
            for_width(width_of(0), gather)
            with pe.Fori(0, E) as e:
                width, next_width = width_of(e), width_of(e + 1)

                def gate_up(width):
                    for u in range(GU_UNITS):
                        s = landed_of(e, u)
                        w = ring[:, s, :].rearrange("p (f g k n) -> p f g k n", f=2, g=2, k=KD)
                        for f in range(2):
                            j = 2 * u + f
                            if j >= 4:
                                pe.wait_ge(e_a, e * NFE + j - 3)
                            for g in range(2):
                                for k in range(KD):
                                    last = pe.matmul(ps[:, j % 4, g * SEQ:g * SEQ + width], w[:, f, g, k, :],
                                                     hTe[:, k, 0:width], start=(k == 0), stop=(k == KD - 1))
                                    if u and (f, g, k) == (0, 0, 0):
                                        last.then_inc(used[(BASE + u - 1) % RING], 1)
                            last.then_inc(e_ps, 1)

                def down(width):
                    for u in range(NFE // 4):
                        s = landed_of(e, GU_UNITS + u)
                        pe.wait_ge(e_a, e * NFE + 4 * u + 4)
                        w = ring[:, s, :].rearrange("p (f n) -> p f n", f=4)
                        for b in range(-(-width // P)):
                            m = min(P, width - b * P)
                            if u == 0 and b == 1:
                                pe.wait_ge(selT_ok, e + 1)
                            for f in range(4):
                                j = 4 * u + f
                                for h in range(2):
                                    last = pe.matmul(ps[0:m, 6 - 2 * b + h, :],
                                                     aT[:, j * SEQ + b * P:j * SEQ + b * P + m],
                                                     w[:, f, h * BANK:(h + 1) * BANK],
                                                     start=(j == 0), stop=(j == NFE - 1))
                        last.then_inc(ye_ps if u == NFE // 4 - 1 else used[s], 1)

                def combine(width):
                    nb = -(-width // P)
                    for i in range(4):
                        for b in range(nb):
                            m = min(P, width - b * P)
                            last = pe.matmul(ps[:, 4 + i, :], selT[0:m, b, (i // 2) * P:(i // 2 + 1) * P],
                                             y_slot[0:m, b, (i % 2) * BANK:(i % 2 + 1) * BANK],
                                             start=(b == 0), stop=(b == nb - 1))
                        last.then_inc(comb_ps, 1)

                pe.wait_ge(hTe_act, e * 4 + 4)
                pe.wait_ge(hTe_dve, e * 4 + 4)
                for_width(width, gate_up)
                pe.wait_ge(selw_ok, e + 1)
                pe.wait_ge(comb_ok, e * 4 + 4)
                for b in range(2):
                    for t in range(TB):
                        last = pe.transpose(ps[:, 4, b * SEQ + t * P:b * SEQ + (t + 1) * P],
                                            selw[:, t, b * P:(b + 1) * P], ident)
                        if (b, t) == (0, 0):
                            last.then_inc(used[(BASE + GU_UNITS - 1) % RING], 1)
                last.then_inc(selT_ps, 1)
                for_width(width, down)
                pe.wait_ge(sel_ok, e + 2)
                for_width(next_width, lambda w: gather(w, (BASE + PER_EXPERT - 1) % RING))
                pe.wait_ge(selT_ok, e + 1)
                pe.wait_ge(ye_act, e * 2 + 2)
                pe.wait_ge(ye_dve, e * 2 + 2)
                for_width(width, combine)


def kernel(**inputs):
    import concourse.bacc as bacc
    from concourse.bass_utils import run_bass_kernel_spmd

    a = {k: np.ascontiguousarray(v) for k, v in inputs.items()}
    f32 = np.float32

    stream = np.empty((UNITS, P, UNIT), f32)
    ada_w = a["ada_w"].reshape(2, KD, P, 6, D)
    cols = [h * HD + i for h in HEAD_ORDER for i in range(HD)]
    w_in = a["e_w_in"][0]
    w_in = np.concatenate([w_in[:, AW:AW + 2 * KW], w_in[:, cols], w_in[:, AW + 2 * KW:]], axis=1)
    w_out = np.concatenate([a["e_w_out"][0][cols], a["e_w_out"][0][AW:]], axis=0)

    def rows(w, j):
        return w[4 * j * P:4 * (j + 1) * P].reshape(-1, P, D).transpose(1, 0, 2).reshape(P, -1)

    def gate_up(g, u, j):
        gu = np.stack([g[:, 2 * j * P:2 * (j + 1) * P], u[:, 2 * j * P:2 * (j + 1) * P]])
        return gu.reshape(2, KD, P, 2, P).transpose(2, 3, 0, 1, 4).reshape(P, UNIT)

    o_in = a["o_w_in"][0].reshape(KD, P, 3, KD, P).transpose(1, 3, 2, 0, 4).reshape(P, 6, UNIT)
    for n, (kind, *j) in enumerate(ORDER):
        if kind == "mod":
            half = ada_w[0, :, :, j[0] // 2, (j[0] % 2) * BANK:(j[0] % 2 + 1) * BANK]
            stream[n] = half.transpose(1, 0, 2).reshape(P, UNIT)
        elif kind == "win":
            stream[n] = w_in[:, BANK * j[0]:BANK * (j[0] + 1)].reshape(KD, P, BANK).transpose(1, 0, 2).reshape(P, UNIT)
        elif kind in ("ada0", "ada1"):
            layer = int(kind[3])
            s = j[0] + 2 * (layer == 0)
            stream[n] = ada_w[layer, 4 * j[1]:4 * j[1] + 4, :, s, :].transpose(1, 0, 2).reshape(P, UNIT)
        elif kind == "wout":
            stream[n] = rows(w_out, j[0])
        elif kind == "gu":
            stream[n] = gate_up(a["e_ffn_gate"][0], a["e_ffn_up"][0], j[0])
        elif kind == "down":
            r = rows(a["e_ffn_down"][0], j[0])
            stream[n, :, :r.shape[1]] = r
            stream[n, :, r.shape[1]:] = 0
        elif kind == "owin":
            stream[n] = o_in[:, j[0]]
        else:
            stream[n] = rows(a["o_w_out"][0], j[0])
    for e in range(E):
        for j in range(GU_UNITS):
            stream[BASE + e * PER_EXPERT + j] = gate_up(a["o_exp_gate"][0, e], a["o_exp_up"][0, e], j)
        for j in range(NFE // 4):
            stream[BASE + e * PER_EXPERT + GU_UNITS + j] = rows(a["o_exp_down"][0, e], j)

    def by_channel(v):
        return np.moveaxis(v.reshape(*v.shape[:-1], KD, P), -1, 0)

    vecs = np.concatenate([
        by_channel(np.stack([a["c"][0], a["c_ctx"]])).transpose(0, 2, 1).reshape(P, -1),
        by_channel(a["ada_b"][0, :2 * D].reshape(2, D)).reshape(P, -1),
        by_channel(a["norm_w"][:, [0, 2]]).reshape(P, -1),
        by_channel(a["o_conv_w"][0]).reshape(P, -1),
        a["o_router"][0].reshape(KD, P, E).transpose(1, 0, 2).reshape(P, -1)], axis=1)
    assert vecs.shape[1] == V_END

    consts = np.concatenate([np.eye(P), np.ones((P, P)), np.tile(E - np.arange(E), (P, 1))], axis=1).astype(f32)
    late = np.concatenate([np.tile(np.arange(SEQ), (P, 1)), np.triu(np.ones((P, P)), 1)], axis=1).astype(f32)
    pos = np.arange(SEQ)
    freq = (10000.0 ** (-np.arange(16, dtype=f32) / f32(16))).astype(f32)
    ang = np.stack([(pos // GRID_W).astype(f32)[:, None] * freq, (pos % GRID_W).astype(f32)[:, None] * freq], axis=1)
    cos, sin = np.cos(ang.astype(np.float64)), np.sin(ang.astype(np.float64))
    rope = np.stack([np.stack([cos, cos], axis=2), np.stack([-sin, sin], axis=2)]).reshape(2, TB, P, HD)
    rope = rope.transpose(2, 0, 1, 3).reshape(P, -1).astype(f32)
    t = 2 * np.pi * np.outer(pos, pos) / SEQ
    g = 2 * np.pi * np.outer(np.arange(FG), np.arange(FG)) / FG
    over_t = np.concatenate([np.cos(t), np.sin(t)], axis=1).reshape(TB, P, 2 * SEQ).transpose(1, 0, 2) / SEQ ** 0.5
    over_g = np.concatenate([np.kron(np.eye(2), np.cos(g)), -np.kron(np.eye(2), np.sin(g))], axis=1) / FG ** 0.5
    dft = np.concatenate([over_t.reshape(P, -1), over_g], axis=1).astype(f32)
    swap = np.arange(HD).reshape(2, 2, 16)[:, ::-1].reshape(-1)
    gains = np.concatenate([a["e_q_gain"][0], a["e_q_gain"][0][swap], a["e_k_gain"][0], a["e_k_gain"][0][swap]])[None]

    arrays = {
        "stream": stream, "x_in": a["x"][0], "ctx_in": a["ctx"][0], "vecs": vecs, "consts": consts,
        "rope": rope, "dft": dft, "gains": gains, "ada_b": a["ada_b"], "norm_w": a["norm_w"].reshape(8, D),
        "late": late,
    }
    arrays = {k: np.ascontiguousarray(v) for k, v in arrays.items()}
    nc = bacc.Bacc("TRN2", target_bir_lowering=False, num_devices=1)
    args = [nc.dram_tensor(k, v.shape, F32, kind="ExternalInput").ap() for k, v in arrays.items()]
    out = nc.dram_tensor("out", (SEQ, D), F32, kind="ExternalOutput").ap()
    build(nc, *args, out)
    r = run_bass_kernel_spmd(nc, [arrays], core_ids=[0])
    return r.results[0]["out"].reshape(1, SEQ, D)
```

```python
from contextlib import ExitStack

import numpy as np

import concourse.bass as bass
from concourse import mybir

P = 128
D = 1024
KD = D // P
SEQ = 256
TB = SEQ // P
CTX = 256
NKB = (SEQ + CTX) // P
HD = 64
NQ, NKV = 12, 4
PAIRS = NQ // 2
AW, KW, FW = NQ * HD, NKV * HD, 256
FG = 64
GRID_W = 64
D_FF = 2816
NF = D_FF // P
E = 8
DE = 3584
NFE = DE // P
EPS = 1e-6
SCALE = HD ** -0.5
RING = 7
UNIT = 4096
BANK = 512
WIDTHS = (64, 96, 128, 160, 192, 256)
BLOCKS = {64: [(0, 64)], 96: [(0, 64), (64, 32)], 128: [(0, 128)], 160: [(0, 128), (128, 32)],
          192: [(0, 128), (128, 64)], 256: [(0, 128), (128, 128)]}
HEAD_ORDER = [h for g in range(2) for i in range(3) for h in (6 * g + i, 6 * g + 3 + i)]

F32 = mybir.dt.float32
I32 = mybir.dt.int32
ALU = mybir.AluOpType
ACT = mybir.ActivationFunctionType
AX = mybir.AxisListType.X


def stream_order():
    order = [("mod", j) for j in range(4)] + [("win", j) for j in range(3)]
    order += [("ada0", s, h) for s in range(4) for h in range(2)]
    order += [("wout", j) for j in range(2)]
    ada1 = [("ada1", s, h) for s in range(6) for h in range(2)]
    for u in range(NF // 2):
        order.append(("gu", u))
        order += ada1[:2] if u == 0 else ada1[u + 1:u + 2]
    order += [("down", j) for j in range(-(-NF // 4))]
    order += [("owin", j) for j in range(6)] + [("owout", j) for j in range(2)]
    return order


ORDER = stream_order()
AT = {what: n for n, what in enumerate(ORDER)}
BASE = len(ORDER)
GU_UNITS = NFE // 2
PER_EXPERT = GU_UNITS + NFE // 4
UNITS = BASE + E * PER_EXPERT
assert PER_EXPERT % RING == 0
LAPS = PER_EXPERT // RING

V_C, V_B0, V_G, V_CONV, V_ROUTER, V_END = 0, 16, 32, 64, 88, 152
C_ID, C_ONE, C_REV, C_PICK, C_END = 0, 128, 256, 264, 266


def build(nc, stream, x_in, ctx_in, vecs, consts, rope, dft, gains, ada_b, norm_w, late, out):
    ctx = ExitStack()
    with ctx:
        def sb(name, shape, dt=F32):
            return ctx.enter_context(nc.sbuf_tensor(name, shape, dt))

        def sem(name):
            return ctx.enter_context(nc.semaphore(name))

        ring = sb("ring", [P, RING, UNIT])
        x = sb("x", [P, TB, D])
        hT = sb("hT", [P, KD, SEQ])
        xn = sb("xn", [P, TB, D])
        aT = sb("aT", [P, NFE * SEQ])
        hTe = sb("hTe", [P, KD, SEQ])
        acc = sb("acc", [P, 6 * D])
        gg = sb("gg", [P, 2, D])
        vec = sb("vec", [P, V_END])
        cst = sb("cst", [P, C_END])
        silu_c = sb("silu_c", [P, KD, 2])
        ab = sb("ab", [P, 5, 2, KD])
        mods0 = sb("mods0", [P, 2, KD, 2])
        stat = sb("stat", [P, 128])
        eps = sb("eps", [P, 1])
        width_at = sb("width_at", [1, E + 1], I32)
        ps = ctx.enter_context(nc.psum_tensor("ps", [P, 8, BANK], F32))

        ident, ones, rev = cst[:, C_ID:C_ID + P], cst[:, C_ONE:C_ONE + P], cst[:, C_REV:C_REV + E]
        pick = cst[:, C_PICK:C_PICK + 2]
        ctx_x = hTe[:, :, :].rearrange("p k t -> p (k t)").rearrange("p (b d) -> p b d", b=TB)
        hTc = acc[:, 4096:6144].rearrange("p (k t) -> p k t", k=KD)
        kz = acc[:, 4096:6144].rearrange("p (j t) -> p j t", j=NKV)
        mod_part = xn[:, :, :].rearrange("p b (h n) -> p (b h) n", h=2)
        qT = hTe[:, 0:PAIRS, :]
        mixT = hT
        q_tok = aT[:, 0:1536].rearrange("p (b n) -> p b n", b=TB)
        k_tok = aT[:, 1536:2560].rearrange("p (b n) -> p b n", b=NKB)
        probs = aT[:, 0:2048].rearrange("p (r n) -> p r n", r=4)
        probsT = aT[:, 3584:5632].rearrange("p (r n) -> p r n", r=4)
        v_tok = aT[:, 2560:3584].rearrange("p (b n) -> p b n", b=NKB)
        f_tok = aT[:, 3584:4096].rearrange("p (b n) -> p b n", b=TB)
        dftL = aT[:, 4096:5120].rearrange("p (b n) -> p b n", b=TB)
        dftD = aT[:, 5120:5376].rearrange("p (b n) -> p b n", b=2)
        roped = aT[:, 5376:5888]
        rope_t = aT[:, 5888:6400].rearrange("p (w c b n) -> p w c b n", w=2, c=2, b=TB)
        gain_t = aT[:, 6400:6656].rearrange("p (w c n) -> p w c n", w=2, c=2)
        rotated = aT[:, 6656:7168]
        fA = [roped, rotated]
        gated = hTe[:, 0:4, :]
        gated_e = hT[:, 0:4, :].rearrange("p (r k) t -> p r (k t)", r=2)
        a_rows = hT[:, 4:8, :].rearrange("p (r k) t -> p r (k t)", r=2)
        aT_e = aT[:, :].rearrange("p (u b n) -> p u b n", b=2, n=256)
        conv_in = hTe[:, :, :].rearrange("p k t -> p (k t)")[:, 0:2 * (SEQ + 2)].rearrange("p (r n) -> p r n", r=2)
        conv_c = hTe[:, 4:6, :]
        conv_s = hTe[:, 6:8, :]
        y_sum = acc[:, 0:2048].rearrange("p (b d) -> p b d", b=TB)
        y_slot = acc[:, 2048:4096].rearrange("p (b d) -> p b d", b=2)
        sel = acc[:, 4096:4608].rearrange("p (b s) -> p b s", b=TB)
        selw = acc[:, 4608:5120].rearrange("p (b s) -> p b s", b=TB)
        selT = acc[:, 5120:5632].rearrange("p (b t) -> p b t", b=2)
        iota, before = acc[:, 5632:5888], acc[:, 5888:6016]

        def small(a, n, w):
            return acc[:, 6016 + a:6016 + a + 2 * n].rearrange("p (b e) -> p b e", b=TB)[:, :, 0:w]

        logit, tmp8, first, second, chosen = (small(16 * i, 8, 8) for i in range(5))
        slot_of, weight_of = small(80, 9, 9), small(98, 9, 9)

        landed = [sem(f"landed{s}") for s in range(RING)]
        used = [sem(f"used{s}") for s in range(RING)]
        small_in, x_in_s, ctx_in_s, tables_in = sem("small_in"), sem("x_in"), sem("ctx_in"), sem("tables_in")
        rows_in, bias_in, late_in = sem("rows_in"), sem("bias_in"), sem("late_in")
        acc_zero, tables_ok, psum_zero, eps_ok = sem("acc_zero"), sem("tables_ok"), sem("psum_zero"), sem("eps_ok")
        silu_ok, mod_sums, mod_ok = sem("silu_ok"), sem("mod_sums"), sem("mod_ok")
        dchain, achain, pchain = sem("dve_chain"), sem("act_chain"), sem("pool_chain")
        root, xn_ok, xT_ok, x_ok = sem("root"), sem("xn_ok"), sem("xT_ok"), sem("x_ok")
        hT_act, hT_dve, raw_act, raw_dve = sem("hT_act"), sem("hT_dve"), sem("raw_act"), sem("raw_dve")
        proj, square, ssum, qk_root = sem("proj"), sem("square"), sem("ssum"), sem("qk_root")
        head_ok, v_ok = sem("head_ok"), sem("v_ok")
        kT_ps, kT_ok, fA_ps, fA_ok, qT_ps, qT_ok, f_ps, f_ok = (
            sem(n) for n in ("kT_ps", "kT_ok", "fA_ps", "fA_ok", "qT_ps", "qT_ok", "f_ps", "f_ok"))
        score, negmax, prob, probT_ps, probT_ok, pv, o_ok = (
            sem(n) for n in ("score", "negmax", "prob", "probT_ps", "probT_ok", "pv", "o_ok"))
        y_ps, kz_zero, norm_p, mod_rows, mod_part_ok = (
            sem(n) for n in ("y_ps", "kz_zero", "norm_p", "mod_rows", "mod_part_ok"))
        red_ps, red_ok, ada_acc = sem("red_ps"), sem("red_ok"), sem("ada_acc")
        gu_ps, silu_out, a_ok = sem("gu_ps"), sem("silu_out"), sem("a_ok")
        c_out, z_ok, conv_ps = sem("c_out"), sem("z_ok"), sem("conv_ps")
        logit_ps, exp_in, exp_out, chosen_ok, rank_ps, width_ok = (
            sem(n) for n in ("logit_ps", "exp_in", "exp_out", "chosen_ok", "rank_ps", "width_ok"))
        sel_ok, selw_ok, gather_ps, hTe_act, hTe_dve = (
            sem(n) for n in ("sel_ok", "selw_ok", "gather_ps", "hTe_act", "hTe_dve"))
        e_ps, e_silu, e_a, eT_ps, eT_ok, selT_ps, selT_ok, ye_ps, ye_act, ye_dve, comb_ps, comb_ok = (
            sem(n) for n in ("e_ps", "e_silu", "e_a", "eT_ps", "eT_ok", "selT_ps", "selT_ok", "ye_ps", "ye_act", "ye_dve",
                             "comb_ps", "comb_ok"))
        stored = sem("stored")

        def slot(what):
            return ring[:, AT[what] % RING, :]

        def wait_landed(eng, what):
            n = AT[what]
            eng.wait_ge(landed[n % RING], 16 * (n // RING + 1))

        def used_up(ins, what):
            ins.then_inc(used[AT[what] % RING], 1)

        def pre_stat(norm, b):
            c = 4 * (TB * norm + b)
            return stat[:, c:c + 1], stat[:, c + 1:c + 2], stat[:, c + 2:c + 3]

        def post_stat(norm, b):
            c = 40 + 3 * (TB * norm + b)
            return stat[:, c:c + 1], stat[:, c + 1:c + 2], stat[:, c + 2:c + 3]

        HEADS = [4, 4, 4, 4, 8, 8, 4, 4]
        hstat = sb("hstat", [P, 3, 40])
        att = sb("att", [P, 3, TB * NQ])
        rt = sb("rt", [P, 8, TB])

        def hcols(i, blk):
            c = sum(HEADS[:blk])
            return hstat[:, i, c:c + HEADS[blk]]

        def y_bank(b):
            return ps[:, 4 + 2 * b:6 + 2 * b, :]

        block = ctx.enter_context(nc.Block())

        @block.sync
        def _(sp):
            for s in range(RING):
                sp.dma_start(ring[:, s, :], stream[s, :, :]).then_inc(landed[s], 16)
            with sp.Fori(1, UNITS // RING) as lap:
                for s in range(RING):
                    sp.wait_ge(used[s], lap)
                    sp.dma_start(ring[:, s, :], stream[lap * RING + s, :, :]).then_inc(landed[s], 16)
            for s in range(UNITS % RING):
                sp.wait_ge(used[s], UNITS // RING)
                sp.dma_start(ring[:, s, :], stream[UNITS - UNITS % RING + s, :, :]).then_inc(landed[s], 16)

        @block.gpsimd
        def _(pool):
            pool.memset(acc[:, 0:4096], 0.0).then_inc(pchain, 1)
            pool.dma_start(dftL, dft[:, 0:1024].rearrange("p (b n) -> p b n", b=TB)).then_inc(tables_in, 16)
            pool.dma_start(dftD, dft[:, 1024:1280].rearrange("p (b n) -> p b n", b=2)).then_inc(tables_in, 16)
            pool.dma_start(rope_t.rearrange("p w c b n -> p (w c b n)"), rope).then_inc(tables_in, 16)
            pool.dma_start(gain_t.rearrange("p w c n -> p (w c n)"), gains.to_broadcast([P, 256])).then_inc(tables_in, 16)
            pool.wait_ge(pchain, 1)
            pool.dma_start(acc[0:1, 0:4096], ada_b[0:1, 2048:6144]).then_inc(bias_in, 16)
            for i in range(2):
                pool.dma_start(gg[:, i, :], norm_w[2 * i + 1:2 * i + 2, :].to_broadcast([P, D])).then_inc(rows_in, 16)
            pool.wait_ge(proj, 4)
            pool.memset(kz, 0.0).then_inc(kz_zero, 1)
            pool.wait_ge(red_ps, 5)
            pool.wait_ge(score, TB * NQ)
            pool.wait_ge(f_ps, 1)
            pool.memset(acc[:, :], 0.0).then_inc(pchain, 1)
            pool.wait_ge(pchain, 2)
            pool.dma_start(acc[0:1, :], ada_b[1:2, :]).then_inc(bias_in, 16)
            pool.wait_ge(x_ok, 2 * TB)
            for i in range(2):
                pool.dma_start(gg[:, i, :], norm_w[4 + 2 * i + 1:4 + 2 * i + 2, :].to_broadcast([P, D])).then_inc(rows_in, 16)
            pool.wait_ge(red_ps, 10)
            pool.dma_start(acc[:, 5632:6016], late).then_inc(late_in, 16)

        @block.scalar
        def _(act):
            links = [0]

            def link(ins):
                links[0] += 1
                ins.then_inc(achain, 1)
                act.wait_ge(achain, links[0])

            def rms(src, junk, st, n):
                link(act.activation(junk, src, ACT.Square, accum_out=st[0]))
                act.activation(st[1], st[0], ACT.Sqrt, bias=eps[:, 0:1], scale=1.0 / n).then_inc(root, 1)

            act.dma_start(vec[:, :], vecs).then_inc(small_in, 16)
            act.dma_start(cst[:, :], consts).then_inc(small_in, 16)
            act.dma_start(x[:, :, :], x_in.rearrange("(b p) d -> p b d", p=P)).then_inc(x_in_s, 16)
            act.dma_start(ctx_x, ctx_in.rearrange("(b p) d -> p b d", p=P)).then_inc(ctx_in_s, 16)
            act.wait_ge(small_in, 32)
            act.activation(silu_c[:, :, :], vec[:, V_C:V_C + 2 * KD].rearrange("p (k v) -> p k v", v=2),
                           ACT.Silu).then_inc(silu_ok, 1)
            act.wait_ge(eps_ok, 1)
            act.wait_ge(x_in_s, 16)
            for b in range(TB):
                rms(x[:, b, :], xn[:, b, :], pre_stat(0, b), D)
            act.wait_ge(ctx_in_s, 16)
            for b in range(TB):
                rms(ctx_x[:, b, :], acc[:, 4096 + D * b:4096 + D * (b + 1)], pre_stat(1, b), D)
            act.wait_ge(xT_ok, TB)
            for j in range(4):
                act.activation(hT[:, 2 * j:2 * j + 2, :].rearrange("p k t -> p (k t)"), ps[:, j, :],
                               ACT.Copy).then_inc(raw_act, 1)
            for j in range(4):
                act.wait_ge(mod_rows, j + 1)
                act.activation(mod_part[:, j, :], ps[:, j, :], ACT.Copy).then_inc(mod_part_ok, 1)
            act.wait_ge(mod_ok, 1)
            act.wait_ge(raw_dve, 4)
            for k in range(KD):
                act.activation(hTc[:, k, :], hTc[:, k, :], ACT.Identity, bias=ab[:, 1, 1, k:k + 1],
                               scale=ab[:, 1, 0, k:k + 1]).then_inc(hT_act, 1)
            for blk in range(8):
                nh = HEADS[blk]
                act.wait_ge(proj, blk + 1)
                if blk < NKB:
                    dst = k_tok[:, blk, :]
                else:
                    dst = q_tok[:, blk % 2, (0 if blk < 6 else 512):(512 if blk < 6 else 768)]
                act.activation(dst, ps[:, blk, 0:nh * HD], ACT.Square).then_inc(square, 1)
                if blk < NKB:
                    act.activation(v_tok[:, blk, :], ps[:, blk, 256:512], ACT.Copy).then_inc(v_ok, 1)
                elif blk >= 6:
                    act.activation(f_tok[:, blk % 2, :], ps[:, blk, 256:512], ACT.Copy).then_inc(v_ok, 1)
                act.wait_ge(ssum, blk + 1)
                act.activation(hcols(1, blk), hcols(0, blk), ACT.Sqrt, bias=eps[:, 0:1],
                               scale=1.0 / HD).then_inc(qk_root, 1)
            act.wait_ge(kz_zero, 1)
            act.wait_ge(kT_ps, 2)
            for j in range(2):
                for a in range(2):
                    rows = slice(a * HD, (a + 1) * HD)
                    act.activation(kz[rows, 2 * j + a, :], ps[rows, j, :], ACT.Copy).then_inc(kT_ok, 1)
            act.wait_ge(qT_ps, 1)
            for j in range(3):
                act.activation(qT[:, 2 * j:2 * j + 2, :].rearrange("p k t -> p (k t)"), ps[:, 4 + j, :],
                               ACT.Copy).then_inc(qT_ok, 1)
            act.wait_ge(f_ps, 1)
            act.activation(mixT[:, 6:8, :].rearrange("p k t -> p (k t)"), ps[:, 7, :], ACT.Copy).then_inc(f_ok, 1)
            for n in range(TB * NQ + 3):
                m = n - 3
                if m >= 0:
                    act.wait_ge(probT_ps, m + 1)
                    if m >= 4:
                        act.wait_ge(pv, (m - 4) // 2 + 1)
                    act.activation(probsT[:, m % 4, :], ps[:, 4 + m % 2, :], ACT.Copy).then_inc(probT_ok, 1)
                if n < TB * NQ:
                    act.wait_ge(negmax, n + 1)
                    if n >= 4:
                        act.wait_ge(probT_ps, n - 3)
                    act.activation(probs[:, n % 4, :], ps[:, n % 4, :], ACT.Exp, bias=att[:, 0, n:n + 1],
                                   accum_out=att[:, 1, n:n + 1]).then_inc(prob, 1)

            def post_pre(post, pre):
                for b in range(TB):
                    act.wait_ge(y_ps, TB * post + b + 1)
                    rms(y_bank(b).rearrange("p a n -> p (a n)"), xn[:, b, :], post_stat(post, b), D)
                    act.wait_ge(x_ok, TB * post + b + 1)
                    rms(x[:, b, :], xn[:, b, :], pre_stat(pre, b), D)
                act.wait_ge(xT_ok, TB * (pre + 1))
                for k in range(KD // 2):
                    act.activation(hT[:, k, :], ps[:, k // 2, (k % 2) * SEQ:(k % 2 + 1) * SEQ], ACT.Identity, bias=ab[:, pre, 1, k:k + 1],
                                   scale=ab[:, pre, 0, k:k + 1]).then_inc(hT_act, 1)

            post_pre(0, 2)
            for j in range(NF):
                act.wait_ge(gu_ps, j + 1)
                act.activation(gated[:, j % 4, :], ps[:, j % 4, 0:SEQ], ACT.Silu).then_inc(silu_out, 1)
            post_pre(1, 3)
            for j in range(KD):
                act.wait_ge(conv_ps, j + 1)
                if j >= 2:
                    act.wait_ge(z_ok, j - 1)
                act.activation(conv_c[:, j % 2, :], ps[:, 2 * (j % 2), SEQ:2 * SEQ], ACT.Copy).then_inc(c_out, 1)
            post_pre(2, 4)
            act.wait_ge(exp_in, 1)
            act.activation(rt[:, 4, :], rt[:, 3, :], ACT.Exp).then_inc(exp_out, 1)

            def take_gather(count):
                for k in range(KD // 2):
                    if k % 2 == 0:
                        act.wait_ge(gather_ps, count + k // 2 + 1)
                    act.activation(hTe[:, k, :], ps[:, k // 2, (k % 2) * SEQ:(k % 2 + 1) * SEQ], ACT.Identity,
                                   bias=ab[:, 4, 1, k:k + 1], scale=ab[:, 4, 0, k:k + 1]).then_inc(hTe_act, 1)

            take_gather(0)
            with act.Fori(0, E) as e:
                def take_turned(u):
                    act.wait_ge(eT_ps, e * GU_UNITS + u + 1)
                    act.activation(aT_e[:, u, :, :].rearrange("p b n -> p (b n)"), ps[:, 6 + u % 2, :],
                                   ACT.Copy).then_inc(eT_ok, 1)

                for u in range(GU_UNITS):
                    act.wait_ge(e_ps, e * GU_UNITS + u + 1)
                    q = 2 * (u % 2)
                    gate = ps[:, q:q + 2, :].rearrange("p b (c g n) -> p (b c) g n", c=2, g=2)[:, :, 0, :]
                    act.activation(gated_e[:, u % 2, :].rearrange("p (c n) -> p c n", c=4), gate,
                                   ACT.Silu).then_inc(e_silu, 1)
                    if u:
                        take_turned(u - 1)
                    if u == 5:
                        act.wait_ge(selT_ps, e + 1)
                        act.activation(selT[:, :, :].rearrange("p b t -> p (b t)"), ps[:, 4, :],
                                       ACT.Copy).then_inc(selT_ok, 1)
                take_turned(GU_UNITS - 1)
                act.wait_ge(ye_ps, e + 1)
                for b in range(2):
                    act.activation(y_slot[:, b, 0:BANK], ps[:, 4 + 2 * b, :], ACT.Copy).then_inc(ye_act, 1)
                take_gather(e * 4 + 4)
            for b in range(TB):
                act.wait_ge(comb_ok, 4 * E + 2 * b + 2)
                rms(y_sum[:, b, :], xn[:, b, :], post_stat(3, b), D)
            for b in range(TB):
                act.wait_ge(x_ok, 3 * TB + b + 1)
                act.dma_start(out[b * P:(b + 1) * P, :], x[:, b, :]).then_inc(stored, 16)
            act.wait_ge(stored, 16 * TB)

        @block.vector
        def _(dve):
            links = [0]

            def link(ins):
                links[0] += 1
                ins.then_inc(dchain, 1)
                dve.wait_ge(dchain, links[0])

            dve.memset(eps[:, :], EPS).then_inc(eps_ok, 1)
            dve.memset(ps[:, :, :], 0.0).then_inc(psum_zero, 1)

            roots = [0]

            def norm_rows(src, dst, st):
                roots[0] += 1
                dve.wait_ge(root, roots[0])
                link(dve.reciprocal(st[2], st[1]))
                dve.tensor_scalar(dst, src, st[2], None, ALU.mult).then_inc(xn_ok, 1)

            dve.wait_ge(x_in_s, 16)
            for b in range(TB):
                norm_rows(x[:, b, :], xn[:, b, :], pre_stat(0, b))
            dve.wait_ge(ctx_in_s, 16)
            for b in range(TB):
                norm_rows(ctx_x[:, b, :], ctx_x[:, b, :], pre_stat(1, b))
            dve.wait_ge(xT_ok, 2 * TB)
            for j in range(4):
                dve.tensor_copy(hTc[:, 2 * j:2 * j + 2, :].rearrange("p k t -> p (k t)"),
                                ps[:, 4 + j, :]).then_inc(raw_dve, 1)
            dve.wait_ge(tables_in, 64)
            for w in range(2):
                for c in range(2):
                    last = dve.tensor_tensor(rope_t[:, w, c, :, :], rope_t[:, w, c, :, :],
                                             gain_t[:, w, c:c + 1, :].to_broadcast([P, TB, HD]), ALU.mult)
            link(last)
            dve.wait_ge(small_in, 32)
            dve.wait_ge(mod_sums, 1)
            b0 = vec[:, V_B0:V_B0 + 16]
            link(dve.tensor_tensor(mods0[:, :, :, :].rearrange("p s k v -> p (s k) v"),
                                   ps[:, 4, 0:32].rearrange("p (m v) -> p m v", v=2),
                                   b0.unsqueeze(2).to_broadcast([P, 16, 2]), ALU.add))
            for v in range(2):
                dve.tensor_copy(ab[:, v, 1, :], mods0[:, 0, :, v])
                last = dve.scalar_tensor_tensor(out=ab[:, v, 0, :], in0=mods0[:, 1, :, v], scalar=1.0,
                                                in1=vec[:, V_G:V_G + KD], op0=ALU.add, op1=ALU.mult)
            last.then_inc(mod_ok, 1)
            dve.wait_ge(mod_ok, 1)
            dve.wait_ge(raw_act, 4)
            for k in range(KD):
                dve.tensor_scalar(hT[:, k, :], hT[:, k, :], ab[:, 0, 0, k:k + 1], ab[:, 0, 1, k:k + 1],
                                  ALU.mult, ALU.add).then_inc(hT_dve, 1)

            def ada_unit(layer, s, h):
                what = (f"ada{layer}", s, h)
                if s == 0 and h == 0:
                    dve.wait_ge(bias_in, 16 * (layer + 1))
                wait_landed(dve, what)
                dst = acc[:, s * D:(s + 1) * D]
                for k in range(4):
                    last = dve.scalar_tensor_tensor(out=dst, in0=slot(what)[:, k * D:(k + 1) * D],
                                                    scalar=silu_c[:, 4 * h + k, 0:1], in1=dst,
                                                    op0=ALU.mult, op1=ALU.add)
                    if k < 3:
                        link(last)
                used_up(last, what)
                n = AT[what]
                dve.wait_ge(used[n % RING], n // RING + 1)
                dve.sem_inc(ada_acc, 1)

            def head_block(blk):
                nh = HEADS[blk]
                w = 1 if blk < NKB else 0
                if blk < NKB:
                    dst = k_tok[:, blk, :]
                else:
                    dst = q_tok[:, blk % 2, (0 if blk < 6 else 512):(512 if blk < 6 else 768)]
                heads = dst.rearrange("p (h d) -> p h d", d=HD)
                dve.wait_ge(square, blk + 1)
                dve.tensor_reduce(hcols(0, blk), heads, AX, ALU.add).then_inc(ssum, 1)
                dve.wait_ge(qk_root, blk + 1)
                link(dve.reciprocal(hcols(2, blk), hcols(1, blk)))
                link(dve.tensor_tensor(heads, ps[:, blk, 0:nh * HD].rearrange("p (h d) -> p h d", d=HD),
                                       hcols(2, blk).unsqueeze(2).to_broadcast([P, nh, HD]), ALU.mult))
                if 2 <= blk < NKB:
                    dve.tensor_tensor(heads, heads, gain_t[:, 1, 0:1, :].to_broadcast([P, nh, HD]),
                                      ALU.mult).then_inc(head_ok, 1)
                    return
                b = blk % 2
                dve.tensor_tensor(roped[:, 0:nh * HD].rearrange("p (h d) -> p h d", d=HD), heads,
                                  rope_t[:, w, 0, b:b + 1, :].to_broadcast([P, nh, HD]), ALU.mult)
                for a in range(2):
                    part = dst.rearrange("p (h x a d) -> p h x a d", x=2, a=2, d=16)[:, :, :, 1 - a, :]
                    to = rotated[:, 0:nh * HD].rearrange("p (h x a d) -> p h x a d", x=2, a=2, d=16)[:, :, :, a, :]
                    tab = rope_t[:, w, 1, b, :].rearrange("p (x a d) -> p x a d", x=2, a=2)[:, :, a, :]
                    last = dve.tensor_tensor(to, part, tab.unsqueeze(1).to_broadcast([P, nh, 2, 16]), ALU.mult)
                link(last)
                dve.tensor_tensor(dst, roped[:, 0:nh * HD], rotated[:, 0:nh * HD], ALU.add).then_inc(head_ok, 1)
                dve.wait_ge(head_ok, blk + 1)

            for blk in range(NKB):
                head_block(blk)
            units0 = [(s, h) for s in range(4) for h in range(2)]
            for n, u in enumerate(units0):
                ada_unit(0, *u)
                if n == 0:
                    head_block(4)
                    head_block(5)
                if n == 3:
                    head_block(6)
                    head_block(7)
                    dve.wait_ge(fA_ps, 1)
                    for j in range(2):
                        dve.tensor_copy(fA[j], ps[:, 2 + j, :]).then_inc(fA_ok, 1)

            for n in range(TB * NQ + 6):
                if n < TB * NQ:
                    dve.wait_ge(score, n + 1)
                    dve.tensor_reduce(att[:, 0, n:n + 1], ps[:, n % 4, :], AX, ALU.max,
                                      negate=True).then_inc(negmax, 1)
                m = n - 1
                if 0 <= m < TB * NQ:
                    dve.wait_ge(prob, m + 1)
                    link(dve.reciprocal(att[:, 2, m:m + 1], att[:, 1, m:m + 1]))
                    dve.tensor_scalar(probs[:, m % 4, :], probs[:, m % 4, :], att[:, 2, m:m + 1], None,
                                      ALU.mult).then_inc(norm_p, 1)
                m = n - 6
                if m >= 0 and m % 2:
                    i, b = m // 4, (m // 2) % 2
                    dve.wait_ge(pv, m // 2 + 1)
                    dve.tensor_copy(mixT[:, i, b * P:(b + 1) * P], ps[:, 6 + b, 0:P]).then_inc(o_ok, 1)

            def gate_half(i):
                half = gg[:, i // 2, (i % 2) * BANK:(i % 2 + 1) * BANK]
                dve.tensor_tensor(half, half, ps[:, i, :], ALU.mult).then_inc(red_ok, 1)

            def factors(pre, src, g):
                dve.tensor_copy(ab[:, pre, 1, :], src[:, 0:KD])
                dve.scalar_tensor_tensor(out=ab[:, pre, 0, :], in0=src[:, KD:2 * KD], scalar=1.0,
                                         in1=vec[:, V_G + KD * g:V_G + KD * (g + 1)], op0=ALU.add,
                                         op1=ALU.mult).then_inc(red_ok, 1)

            dve.wait_ge(rows_in, 32)
            for i in range(4):
                dve.wait_ge(red_ps, i + 1)
                gate_half(i)
            dve.wait_ge(red_ps, 5)
            factors(2, ps[:, 0, 0:16], 1)

            def post_pre(post, pre):
                for b in range(TB):
                    st = post_stat(post, b)
                    roots[0] += 1
                    dve.wait_ge(root, roots[0])
                    link(dve.reciprocal(st[2], st[1]))
                    link(dve.scalar_tensor_tensor(out=xn[:, b, :], in0=y_bank(b).rearrange("p a n -> p (a n)"),
                                                  scalar=st[2], in1=gg[:, post % 2, :], op0=ALU.mult, op1=ALU.mult))
                    dve.tensor_tensor(x[:, b, :], x[:, b, :], xn[:, b, :], ALU.add).then_inc(x_ok, 1)
                    norm_rows(x[:, b, :], xn[:, b, :], pre_stat(pre, b))
                dve.wait_ge(xT_ok, TB * (pre + 1))
                for k in range(KD // 2, KD):
                    dve.tensor_scalar(hT[:, k, :], ps[:, k // 2, (k % 2) * SEQ:(k % 2 + 1) * SEQ], ab[:, pre, 0, k:k + 1],
                                      ab[:, pre, 1, k:k + 1], ALU.mult, ALU.add).then_inc(hT_dve, 1)

            post_pre(0, 2)
            units1 = [(s, h) for s in range(6) for h in range(2)]
            for j in range(NF):
                dve.wait_ge(silu_out, j + 1)
                dve.tensor_tensor(aT[:, j * SEQ:(j + 1) * SEQ], gated[:, j % 4, :], ps[:, j % 4, SEQ:2 * SEQ],
                                  ALU.mult).then_inc(a_ok, 1)
                if j % 2:
                    for _ in range(2 if j == 1 else 1):
                        ada_unit(1, *units1.pop(0))
            dve.wait_ge(red_ps, 6)
            factors(3, ps[:, 0, 0:16], 2)
            factors(4, ps[:, 0, 16:32], 3)
            post_pre(1, 3)
            link(dve.memset(conv_in, 0.0))
            for j in range(KD):
                r = j % 2
                dve.wait_ge(c_out, j + 1)
                link(dve.tensor_tensor(conv_in[:, r, 1:SEQ + 1], conv_c[:, r, :], ps[:, 2 * r + 1, 0:SEQ], ALU.mult))
                link(dve.tensor_scalar(conv_s[:, r, :], conv_in[:, r, 0:SEQ], vec[:, V_CONV + j:V_CONV + j + 1],
                                       None, ALU.mult))
                for t in (1, 2):
                    c = V_CONV + KD * t + j
                    link(dve.scalar_tensor_tensor(out=conv_s[:, r, :], in0=conv_in[:, r, t:t + SEQ],
                                                  scalar=vec[:, c:c + 1], in1=conv_s[:, r, :], op0=ALU.mult,
                                                  op1=ALU.add))
                dve.tensor_tensor(aT[:, j * SEQ:(j + 1) * SEQ], conv_s[:, r, :], ps[:, 2 * r, 0:SEQ],
                                  ALU.mult).then_inc(z_ok, 1)
            dve.wait_ge(rows_in, 64)
            for i in range(4):
                dve.wait_ge(red_ps, 7 + i)
                gate_half(i)
            for i in range(4):
                dve.memset(y_sum[:, i // 2, (i % 2) * BANK:(i % 2 + 1) * BANK], 0.0).then_inc(comb_ok, 1)
            post_pre(2, 4)

            dve.wait_ge(late_in, 16)

            def rb(i):
                return rt[:, i, :].unsqueeze(2).to_broadcast([P, TB, E])

            revb = rev.unsqueeze(1).to_broadcast([P, TB, E])
            dve.wait_ge(logit_ps, 1)
            link(dve.tensor_copy(logit, ps[:, 4, 0:TB * E].rearrange("p (b e) -> p b e", b=TB)))

            def top(values, mask, i):
                link(dve.tensor_reduce(rt[:, i, :], values, AX, ALU.max))
                link(dve.tensor_tensor(mask, values, rb(i), ALU.is_equal))
                link(dve.tensor_tensor(mask, mask, revb, ALU.mult))
                link(dve.tensor_reduce(rt[:, 2, :], mask, AX, ALU.max))
                link(dve.tensor_tensor(mask, revb, rb(2), ALU.is_equal))

            top(logit, first, 0)
            link(dve.scalar_tensor_tensor(out=tmp8, in0=first, scalar=-3.0e38, in1=logit, op0=ALU.mult, op1=ALU.add))
            top(tmp8, second, 1)
            dve.tensor_tensor(chosen, first, second, ALU.add).then_inc(chosen_ok, 1)
            dve.tensor_tensor(rt[:, 3, :], rt[:, 1, :], rt[:, 0, :], ALU.subtract).then_inc(exp_in, 1)
            dve.wait_ge(exp_out, 1)
            link(dve.tensor_scalar(rt[:, 5, :], rt[:, 4, :], 1.0, None, ALU.add))
            link(dve.reciprocal(rt[:, 6, :], rt[:, 5, :]))
            link(dve.tensor_tensor(rt[:, 7, :], rt[:, 4, :], rt[:, 6, :], ALU.mult))
            link(dve.tensor_tensor(first, first, rb(6), ALU.mult))
            link(dve.tensor_tensor(second, second, rb(7), ALU.mult))
            link(dve.memset(weight_of, 0.0))
            link(dve.memset(slot_of, -1.0))
            link(dve.tensor_tensor(weight_of[:, :, 0:E], first, second, ALU.add))
            dve.wait_ge(rank_ps, 1)
            link(dve.scalar_tensor_tensor(out=slot_of[:, :, 0:E], in0=ps[:, 5, 0:TB * E].rearrange("p (b e) -> p b e", b=TB),
                                          scalar=1.0, in1=chosen, op0=ALU.add, op1=ALU.mult))
            link(dve.tensor_scalar(slot_of[:, :, 0:E], slot_of[:, :, 0:E], -1.0, None, ALU.add))
            count = ps[0:1, 6, 0:E]
            wsum = hstat[0:1, 0, 0:E]
            link(dve.tensor_scalar(wsum, count, float(WIDTHS[0]), None, ALU.is_gt))
            for w in WIDTHS[1:-1]:
                link(dve.scalar_tensor_tensor(out=wsum, in0=count, scalar=float(w), in1=wsum, op0=ALU.is_gt, op1=ALU.add))
            link(dve.memset(width_at[:, :], 0))
            dve.tensor_copy(width_at[0:1, 0:E], wsum).then_inc(width_ok, 1)

            def select(e, weighted):
                for b in range(TB):
                    at = slot_of[:, b, bass.ds(e, 1)]
                    if weighted:
                        last = dve.tensor_scalar(selw[:, b, :], iota, at, weight_of[:, b, bass.ds(e, 1)],
                                                 ALU.is_equal, ALU.mult)
                    else:
                        last = dve.tensor_scalar(sel[:, b, :], iota, at, None, ALU.is_equal)
                last.then_inc(selw_ok if weighted else sel_ok, 1)

            def take_gather(count):
                for k in range(KD // 2, KD):
                    if k % 2 == 0:
                        dve.wait_ge(gather_ps, count + k // 2 + 1)
                    dve.tensor_scalar(hTe[:, k, :], ps[:, k // 2, (k % 2) * SEQ:(k % 2 + 1) * SEQ],
                                      ab[:, 4, 0, k:k + 1], ab[:, 4, 1, k:k + 1], ALU.mult,
                                      ALU.add).then_inc(hTe_dve, 1)

            select(0, False)
            select(0, True)
            take_gather(0)
            with dve.Fori(0, E) as e:
                dve.wait_ge(gather_ps, e * 4 + 4)
                select(e + 1, False)
                for u in range(GU_UNITS):
                    dve.wait_ge(e_silu, e * GU_UNITS + u + 1)
                    q = 2 * (u % 2)
                    up = ps[:, q:q + 2, :].rearrange("p b (c g n) -> p (b c) g n", c=2, g=2)[:, :, 1, :]
                    dve.tensor_tensor(a_rows[:, u % 2, :].rearrange("p (c n) -> p c n", c=4),
                                      gated_e[:, u % 2, :].rearrange("p (c n) -> p c n", c=4), up,
                                      ALU.mult).then_inc(e_a, 1)
                    if u == 7:
                        dve.wait_ge(selT_ps, e + 1)
                        select(e + 1, True)
                dve.wait_ge(ye_ps, e + 1)
                for b in range(2):
                    dve.tensor_copy(y_slot[:, b, BANK:2 * BANK], ps[:, 5 + 2 * b, :]).then_inc(ye_dve, 1)
                take_gather(e * 4 + 4)
                for i in range(4):
                    dve.wait_ge(comb_ps, e * 4 + i + 1)
                    part = y_sum[:, i // 2, (i % 2) * BANK:(i % 2 + 1) * BANK]
                    dve.tensor_tensor(part, part, ps[:, 4 + i, :], ALU.add).then_inc(comb_ok, 1)
            for b in range(TB):
                st = post_stat(3, b)
                roots[0] += 1
                dve.wait_ge(root, roots[0])
                link(dve.reciprocal(st[2], st[1]))
                link(dve.scalar_tensor_tensor(out=xn[:, b, :], in0=y_sum[:, b, :], scalar=st[2],
                                              in1=gg[:, 1, :], op0=ALU.mult, op1=ALU.mult))
                dve.tensor_tensor(x[:, b, :], x[:, b, :], xn[:, b, :], ALU.add).then_inc(x_ok, 1)

        @block.tensor
        def _(pe):
            def turn_rows(src, bank0, order, before=None):
                for b in range(TB):
                    pe.wait_ge(xn_ok, order * TB + b + 1)
                    for k in range(KD):
                        if b == 0 and k == 1 and before:
                            used_up(last, before)
                        last = pe.transpose(ps[:, bank0 + k // 2, (k % 2) * SEQ + b * P:(k % 2) * SEQ + (b + 1) * P],
                                            src[:, b, k * P:(k + 1) * P], ident)
                    last.then_inc(xT_ok, 1)

            pe.wait_ge(small_in, 32)
            pe.wait_ge(psum_zero, 1)
            turn_rows(xn, 0, 0)
            turn_rows(ctx_x, 4, 1)
            pe.wait_ge(silu_ok, 1)
            pe.wait_ge(raw_act, 4)
            pe.wait_ge(raw_dve, 1)

            def mod_columns(j):
                pe.wait_ge(mod_part_ok, j + 1)
                for m in range(4):
                    c = 2 * (4 * j + m)
                    last = pe.matmul(ps[:, 4, c:c + 2], mod_part[:, j, m * P:(m + 1) * P], pick,
                                     start=True, stop=True)
                return last

            for j in range(4):
                wait_landed(pe, ("mod", j))
                w = slot(("mod", j)).rearrange("p (k n) -> p k n", k=KD)
                for half in range(2):
                    for r in range(4):
                        last = pe.matmul(ps[32 * r:32 * r + 2, j, :], silu_c[:, 2 * r + half, :],
                                         w[:, 2 * r + half, :], start=(half == 0), stop=(half == 1))
                last.then_inc(mod_rows, 1)
                if j:
                    used_up(mod_columns(j - 1), ("mod", j - 1))
            mod_columns(3).then_inc(mod_sums, 1)
            for blk in range(8):
                unit = ("win", 0 if blk < 4 else 1 if blk < 6 else 2)
                lhs = hTc if blk in (2, 3) else hT
                b = blk % 2
                wait_landed(pe, unit)
                w = slot(unit).rearrange("p (k n) -> p k n", k=KD)
                if blk == 0:
                    pe.wait_ge(mod_part_ok, 4)
                if blk == 4:
                    pe.wait_ge(raw_dve, 4)
                for k in range(KD):
                    if blk == 0:
                        pe.wait_ge(hT_dve, k + 1)
                    if blk == 2:
                        pe.wait_ge(hT_act, k + 1)
                    last = pe.matmul(ps[:, blk, :], lhs[:, k, b * P:(b + 1) * P], w[:, k, :],
                                     start=(k == 0), stop=(k == KD - 1))
                    if k == 0 and blk in (0, 4, 6):
                        used_up(last, {0: ("mod", 3), 4: ("win", 0), 6: ("win", 1)}[blk])
                last.then_inc(proj, 1)
            pe.wait_ge(head_ok, 4)
            pe.wait_ge(v_ok, 4)
            for j in range(2):
                for b in range(NKB):
                    last = pe.transpose(ps[:, j, b * P:(b + 1) * P], k_tok[:, b, j * P:(j + 1) * P], ident)
                    if j == 0 and b == 0:
                        used_up(last, ("win", 2))
                last.then_inc(kT_ps, 1)
            pe.wait_ge(v_ok, 6)
            pe.wait_ge(tables_in, 64)
            for j in range(2):
                for b in range(TB):
                    last = pe.matmul(ps[:, 2 + j, :], f_tok[:, b, j * P:(j + 1) * P], dftL[:, b, :],
                                     start=(b == 0), stop=(b == TB - 1))
            last.then_inc(fA_ps, 1)
            pe.wait_ge(head_ok, 8)
            for i in range(PAIRS):
                for b in range(TB):
                    last = pe.transpose(ps[:, 4 + i // 2, (i % 2) * SEQ + b * P:(i % 2) * SEQ + (b + 1) * P],
                                        q_tok[:, b, i * P:(i + 1) * P], ident)
            last.then_inc(qT_ps, 1)
            pe.wait_ge(fA_ok, 2)
            for j in range(2):
                for c in range(2):
                    last = pe.matmul(ps[:, 7, j * SEQ:(j + 1) * SEQ], dftD[:, c, :], fA[j][:, c * SEQ:(c + 1) * SEQ],
                                     start=(c == 0), stop=(c == 1))
            last.then_inc(f_ps, 1)
            pe.wait_ge(kT_ok, 4)
            pe.wait_ge(qT_ok, 3)
            pe.wait_ge(f_ok, 1)
            for n in range(TB * NQ + 5):
                if n < TB * NQ:
                    i, b, a = n // 4, (n // 2) % 2, n % 2
                    if n >= 4:
                        pe.wait_ge(prob, n - 3)
                    pe.matmul(ps[:, n % 4, :], qT[:, i, b * P:(b + 1) * P], kz[:, 2 * (i // 3) + a, :],
                              start=True, stop=True).then_inc(score, 1)
                m = n - 3
                if 0 <= m < TB * NQ:
                    pe.wait_ge(norm_p, m + 1)
                    if m >= 2:
                        pe.wait_ge(probT_ok, m - 1)
                    for b in range(NKB):
                        last = pe.transpose(ps[:, 4 + m % 2, b * P:(b + 1) * P],
                                            probs[:, m % 4, b * P:(b + 1) * P], ident)
                    last.then_inc(probT_ps, 1)
                m = n - 5
                if m >= 0 and m % 2:
                    i, b = m // 4, (m // 2) % 2
                    pe.wait_ge(probT_ok, m + 1)
                    if m >= 5:
                        pe.wait_ge(o_ok, m // 2 - 1)
                    for kb in range(NKB):
                        for a in range(2):
                            kv = 2 * (i // 3) + a
                            last = pe.matmul(ps[a * HD:(a + 1) * HD, 6 + b, 0:P], v_tok[:, kb, kv * HD:(kv + 1) * HD],
                                             probsT[:, (m - 1 + a) % 4, kb * P:(kb + 1) * P],
                                             start=(kb == 0), stop=(kb == NKB - 1))
                    last.then_inc(pv, 1)
            pe.wait_ge(ada_acc, 8)
            pe.wait_ge(prob, TB * NQ)
            for i in range(4):
                c = (3 * D if i >= 2 else 0) + (i % 2) * BANK
                pe.matmul(ps[:, i, :], ones, acc[:, c:c + BANK], start=True, stop=True).then_inc(red_ps, 1)
            pe.wait_ge(red_ok, 1)
            for k in range(16):
                last = pe.matmul(ps[:, 0, k:k + 1], acc[:, D + k * P:D + (k + 1) * P], ones[:, 0:1],
                                 start=True, stop=True)
            last.then_inc(red_ps, 1)

            def project(units, per_unit, nblocks, lhs):
                for b in range(TB):
                    for k in range(nblocks):
                        unit = units[k // per_unit]
                        if b == 0 and k % per_unit == 0:
                            wait_landed(pe, unit)
                        w = slot(unit).rearrange("p (k n) -> p k n", k=per_unit)
                        for h in range(2):
                            last = pe.matmul(ps[:, 4 + 2 * b + h, :], lhs(k)[:, b * P:(b + 1) * P],
                                             w[:, k % per_unit, h * BANK:(h + 1) * BANK],
                                             start=(k == 0), stop=(k == nblocks - 1))
                        if b == TB - 1 and (k % per_unit == per_unit - 1 or k == nblocks - 1) and k < nblocks - 1:
                            used_up(last, unit)
                    last.then_inc(y_ps, 1)

            pe.wait_ge(probT_ok, TB * NQ)
            pe.wait_ge(o_ok, TB * PAIRS)
            project([("wout", 0), ("wout", 1)], 4, KD, lambda k: mixT[:, k, :])
            pe.wait_ge(red_ok, 5)

            def wait_hT(pre, k):
                half = KD // 2
                pe.wait_ge(hT_act if k < half else hT_dve, KD + half * (pre - 2) + k % half + 1)

            turn_rows(xn, 0, 2, ("wout", 1))
            for u in range(NF // 2):
                wait_landed(pe, ("gu", u))
                w = slot(("gu", u)).rearrange("p (f g k n) -> p f g k n", f=2, g=2, k=KD)
                for f in range(2):
                    j = 2 * u + f
                    if j >= 4:
                        pe.wait_ge(a_ok, j - 3)
                    if j == 0:
                        for k in range(KD):
                            wait_hT(2, k)
                    for g in range(2):
                        for k in range(KD):
                            last = pe.matmul(ps[:, j % 4, g * SEQ:(g + 1) * SEQ], w[:, f, g, k, :], hT[:, k, :],
                                             start=(k == 0), stop=(k == KD - 1))
                            if u and (f, g, k) == (0, 0, 0):
                                used_up(last, ("gu", u - 1))
                    last.then_inc(gu_ps, 1)
            pe.wait_ge(ada_acc, 8 + 12)
            pe.wait_ge(a_ok, NF)
            for k in range(32):
                c = (k // 16) * 3 * D + (k % 16) * P
                last = pe.matmul(ps[:, 0, k:k + 1], acc[:, c:c + P], ones[:, 0:1], start=True, stop=True)
                if k == 0:
                    used_up(last, ("gu", NF // 2 - 1))
            last.then_inc(red_ps, 1)
            project([("down", j) for j in range(-(-NF // 4))], 4, NF, lambda k: aT[:, k * SEQ:(k + 1) * SEQ])
            pe.wait_ge(red_ok, 7)
            turn_rows(xn, 0, 3, ("down", -(-NF // 4) - 1))
            for i in range(3 * KD):
                unit = ("owin", i // 4)
                j, part = i // 3, i % 3
                if i % 4 == 0:
                    wait_landed(pe, unit)
                w = slot(unit).rearrange("p (f k n) -> p f k n", f=4, k=KD)
                if part == 0 and j >= 2:
                    pe.wait_ge(z_ok, j - 1)
                if i == 0:
                    for k in range(KD):
                        wait_hT(3, k)
                bank, c = (2 * (j % 2) + 1, 0) if part == 2 else (2 * (j % 2), part * SEQ)
                for k in range(KD):
                    last = pe.matmul(ps[:, bank, c:c + SEQ], w[:, i % 4, k, :], hT[:, k, :],
                                     start=(k == 0), stop=(k == KD - 1))
                    if k == 0 and i and i % 4 == 0:
                        used_up(last, ("owin", i // 4 - 1))
                if part == 2:
                    last.then_inc(conv_ps, 1)
            pe.wait_ge(z_ok, KD)
            pe.sem_inc(used[AT[("owin", 5)] % RING], 1)
            for i in range(4):
                c = (5 if i >= 2 else 2) * D + (i % 2) * BANK
                pe.matmul(ps[:, i, :], ones, acc[:, c:c + BANK], start=True, stop=True).then_inc(red_ps, 1)
            project([("owout", 0), ("owout", 1)], 4, KD, lambda k: aT[:, k * SEQ:(k + 1) * SEQ])
            pe.wait_ge(red_ok, 11)
            turn_rows(xn, 0, 4, ("owout", 1))
            router = vec[:, V_ROUTER:V_ROUTER + KD * E].rearrange("p (k e) -> p k e", e=E)
            for k in range(KD):
                wait_hT(4, k)
            pe.wait_ge(x_ok, 3 * TB)
            for b in range(TB):
                for k in range(KD):
                    last = pe.matmul(ps[:, 4, b * E:(b + 1) * E], hT[:, k, b * P:(b + 1) * P], router[:, k, :],
                                     start=(k == 0), stop=(k == KD - 1))
            last.then_inc(logit_ps, 1)
            pe.wait_ge(chosen_ok, 1)
            pe.wait_ge(late_in, 16)
            pe.matmul(ps[:, 5, 0:E], before, chosen[:, 0, :], start=True, stop=True)
            pe.matmul(ps[:, 5, E:2 * E], ones, chosen[:, 0, :], start=True, stop=False)
            pe.matmul(ps[:, 5, E:2 * E], before, chosen[:, 1, :], start=False, stop=True)
            pe.matmul(ps[0:1, 6, 0:E], ones[:, 0:1], chosen[:, 0, :], start=True, stop=False)
            pe.matmul(ps[0:1, 6, 0:E], ones[:, 0:1], chosen[:, 1, :], start=False, stop=True).then_inc(rank_ps, 1)

            def width_of(at):
                return pe.value_load(width_at[0:1, bass.ds(at, 1)], min_val=0, max_val=len(WIDTHS) - 1)

            def for_width(which, body):
                for i, width in enumerate(WIDTHS):
                    with pe.If(which == i):
                        body(width)

            def gather(width, before=None):
                for j in range(4):
                    for i in range(2):
                        for b in range(TB):
                            last = pe.matmul(ps[:, j, i * SEQ:i * SEQ + width], xn[:, b, (2 * j + i) * P:(2 * j + i + 1) * P],
                                             sel[:, b, 0:width], start=(b == 0), stop=(b == TB - 1))
                            if (j, i, b) == (0, 0, 0) and before is not None:
                                last.then_inc(used[before], 1)
                    last.then_inc(gather_ps, 1)

            def landed_of(e, i):
                n = BASE + i
                pe.wait_ge(landed[n % RING], e * (16 * LAPS) + 16 * (n // RING + 1))
                return n % RING

            pe.wait_ge(width_ok, 1)
            pe.wait_ge(sel_ok, 1)
            for_width(width_of(0), gather)
            with pe.Fori(0, E) as e:
                width, next_width = width_of(e), width_of(e + 1)

                def done_before(width, u):
                    if any(n == 32 for _, n in BLOCKS[width]):
                        return [] if u % 2 else [u - 2, u - 1] if u else []
                    return [u - 1] if u else []

                def turn(width, u):
                    pe.wait_ge(e_a, e * GU_UNITS + u + 1)
                    if u >= 2:
                        pe.wait_ge(eT_ok, e * GU_UNITS + u - 1)
                    for b, (s0, n) in enumerate(BLOCKS[width]):
                        if n == 32 and u % 2 == 0:
                            continue
                        for c in range(2 if n == P else 1):
                            last = pe.transpose(ps[:, 6 + u % 2, b * 256 + c * P:b * 256 + (c + 1) * P],
                                                a_rows[:, u % 2, (2 * b + c) * P:(2 * b + c + 1) * P], ident)
                    last.then_inc(eT_ps, 1)

                def gate_up(width):
                    for u in range(GU_UNITS):
                        landed_of(e, u)
                        if u >= 2:
                            pe.wait_ge(e_a, e * GU_UNITS + u - 1)
                        done, count = done_before(width, u), 0
                        for b, (s0, n) in enumerate(BLOCKS[width]):
                            tiles = P // n
                            if tiles == 4 and u % 2 == 0:
                                continue
                            bank = 2 * (u % 2) + b
                            for k in range(KD):
                                for r in range(tiles):
                                    v = u if tiles < 4 else u - 1 + r // 2
                                    w = ring[:, (BASE + v) % RING, k * 512:(k + 1) * 512]
                                    if tiles > 1:
                                        w = w[:, (r % 2) * 256:(r % 2 + 1) * 256]
                                    last = pe.matmul(ps[n * r:n * (r + 1), bank, 0:(512 if tiles == 1 else 256)],
                                                     hTe[:, k, s0:s0 + n], w, start=(k == 0), stop=(k == KD - 1))
                                    if count < len(done):
                                        last.then_inc(used[(BASE + done[count]) % RING], 1)
                                    count += 1
                        last.then_inc(e_ps, 1)
                        if u == 1:
                            pe.wait_ge(comb_ok, e * 4 + 4)
                        if u:
                            turn(width, u - 1)
                        if u == 5:
                            pe.wait_ge(selw_ok, e + 1)
                            for b, (s0, n) in enumerate(BLOCKS[width]):
                                for t in range(TB):
                                    for r in range(P // n):
                                        last = pe.matmul(ps[n * r:n * (r + 1), 4, b * SEQ + t * P:b * SEQ + (t + 1) * P],
                                                         selw[:, t, s0:s0 + n], ident, start=True, stop=True)
                            last.then_inc(selT_ps, 1)

                def down(width):
                    pe.wait_ge(selT_ok, e + 1)
                    done, count = done_before(width, GU_UNITS), 0
                    for d in range(NFE // 4):
                        s = landed_of(e, GU_UNITS + d)
                        pe.wait_ge(eT_ok, e * GU_UNITS + 2 * d + 2)
                        w = ring[:, s, :].rearrange("p (f n) -> p f n", f=4)
                        for b, (s0, n) in enumerate(BLOCKS[width]):
                            tiles = P // n
                            if d == 0 and b == 1:
                                pe.wait_ge(eT_ok, (e + 1) * GU_UNITS)
                            for h in range(2):
                                for f in range(4):
                                    j, r = 4 * d + f, f % tiles
                                    u = j // 2 if tiles < 4 else 2 * d + 1
                                    c = n * (f % 2 if tiles < 4 else f)
                                    last = pe.matmul(ps[n * r:n * (r + 1), 4 + 2 * b + h, :],
                                                     aT_e[:, u, b, c:c + n], w[:, f, h * BANK:(h + 1) * BANK],
                                                     start=(j < tiles), stop=(j >= NFE - tiles))
                                    if count < len(done):
                                        last.then_inc(used[(BASE + done[count]) % RING], 1)
                                    count += 1
                            if d < NFE // 4 - 1 and b == len(BLOCKS[width]) - 1:
                                last.then_inc(used[s], 1)
                            if d == 0 and b == 0:
                                turn(width, GU_UNITS - 1)
                    last.then_inc(ye_ps, 1)

                def combine(width):
                    for i in range(4):
                        for b in range(len(BLOCKS[width])):
                            last = pe.matmul(ps[:, 4 + i, :], selT[:, b, (i // 2) * P:(i // 2 + 1) * P],
                                             y_slot[:, b, (i % 2) * BANK:(i % 2 + 1) * BANK],
                                             start=(b == 0), stop=(b == len(BLOCKS[width]) - 1))
                        last.then_inc(comb_ps, 1)

                pe.wait_ge(hTe_act, e * 4 + 4)
                pe.wait_ge(hTe_dve, e * 4 + 4)
                for_width(width, gate_up)
                for_width(width, down)
                pe.wait_ge(sel_ok, e + 2)
                for_width(next_width, lambda w: gather(w, (BASE + PER_EXPERT - 1) % RING))
                pe.wait_ge(ye_act, e * 2 + 2)
                pe.wait_ge(ye_dve, e * 2 + 2)
                for_width(width, combine)


def kernel(**inputs):
    import concourse.bacc as bacc
    from concourse.bass_utils import run_bass_kernel_spmd

    a = {k: np.ascontiguousarray(v) for k, v in inputs.items()}
    f32 = np.float32

    stream = np.empty((UNITS, P, UNIT), f32)
    ada_w = a["ada_w"].reshape(2, KD, P, 6, D)
    cols = [h * HD + i for h in HEAD_ORDER for i in range(HD)]
    w_in = a["e_w_in"][0]
    w_in = np.concatenate([w_in[:, AW:AW + 2 * KW], w_in[:, cols], w_in[:, AW + 2 * KW:]], axis=1)
    w_out = np.concatenate([a["e_w_out"][0][cols], a["e_w_out"][0][AW:]], axis=0)

    def rows(w, j):
        return w[4 * j * P:4 * (j + 1) * P].reshape(-1, P, D).transpose(1, 0, 2).reshape(P, -1)

    def gate_up(g, u, j):
        gu = np.stack([g[:, 2 * j * P:2 * (j + 1) * P], u[:, 2 * j * P:2 * (j + 1) * P]])
        return gu.reshape(2, KD, P, 2, P)

    o_in = a["o_w_in"][0].reshape(KD, P, 3, KD, P).transpose(1, 3, 2, 0, 4).reshape(P, 6, UNIT)
    for n, (kind, *j) in enumerate(ORDER):
        if kind == "mod":
            half = ada_w[0, :, :, j[0] // 2, (j[0] % 2) * BANK:(j[0] % 2 + 1) * BANK]
            stream[n] = half.transpose(1, 0, 2).reshape(P, UNIT)
        elif kind == "win":
            stream[n] = w_in[:, BANK * j[0]:BANK * (j[0] + 1)].reshape(KD, P, BANK).transpose(1, 0, 2).reshape(P, UNIT)
        elif kind in ("ada0", "ada1"):
            layer = int(kind[3])
            s = j[0] + 2 * (layer == 0)
            stream[n] = ada_w[layer, 4 * j[1]:4 * j[1] + 4, :, s, :].transpose(1, 0, 2).reshape(P, UNIT)
        elif kind == "wout":
            stream[n] = rows(w_out, j[0])
        elif kind == "gu":
            stream[n] = gate_up(a["e_ffn_gate"][0], a["e_ffn_up"][0], j[0]).transpose(2, 3, 0, 1, 4).reshape(P, UNIT)
        elif kind == "down":
            r = rows(a["e_ffn_down"][0], j[0])
            stream[n, :, :r.shape[1]] = r
            stream[n, :, r.shape[1]:] = 0
        elif kind == "owin":
            stream[n] = o_in[:, j[0]]
        else:
            stream[n] = rows(a["o_w_out"][0], j[0])
    for e in range(E):
        for j in range(GU_UNITS):
            gu = gate_up(a["o_exp_gate"][0, e], a["o_exp_up"][0, e], j)
            stream[BASE + e * PER_EXPERT + j] = gu.transpose(2, 1, 3, 0, 4).reshape(P, UNIT)
        for j in range(NFE // 4):
            stream[BASE + e * PER_EXPERT + GU_UNITS + j] = rows(a["o_exp_down"][0, e], j)

    def by_channel(v):
        return np.moveaxis(v.reshape(*v.shape[:-1], KD, P), -1, 0)

    vecs = np.concatenate([
        by_channel(np.stack([a["c"][0], a["c_ctx"]])).transpose(0, 2, 1).reshape(P, -1),
        by_channel(a["ada_b"][0, :2 * D].reshape(2, D)).reshape(P, -1),
        by_channel(a["norm_w"][:, [0, 2]]).reshape(P, -1),
        by_channel(a["o_conv_w"][0]).reshape(P, -1),
        a["o_router"][0].reshape(KD, P, E).transpose(1, 0, 2).reshape(P, -1)], axis=1)
    assert vecs.shape[1] == V_END

    consts = np.concatenate([np.eye(P), np.ones((P, P)), np.tile(E - np.arange(E), (P, 1)),
                             np.arange(P)[:, None] % 32 == np.arange(2)], axis=1).astype(f32)
    late = np.concatenate([np.tile(np.arange(SEQ), (P, 1)), np.triu(np.ones((P, P)), 1)], axis=1).astype(f32)
    pos = np.arange(SEQ)
    freq = (10000.0 ** (-np.arange(16, dtype=f32) / f32(16))).astype(f32)
    ang = np.stack([(pos // GRID_W).astype(f32)[:, None] * freq, (pos % GRID_W).astype(f32)[:, None] * freq], axis=1)
    cos, sin = np.cos(ang.astype(np.float64)), np.sin(ang.astype(np.float64))
    rope = np.stack([np.stack([cos, cos], axis=2), np.stack([-sin, sin], axis=2)]).reshape(2, TB, P, HD)
    rope = rope.transpose(2, 0, 1, 3).reshape(P, -1)
    rope = np.stack([rope * SCALE, rope], axis=1).reshape(P, -1).astype(f32)
    t = 2 * np.pi * np.outer(pos, pos) / SEQ
    g = 2 * np.pi * np.outer(np.arange(FG), np.arange(FG)) / FG
    over_t = np.concatenate([np.cos(t), np.sin(t)], axis=1).reshape(TB, P, 2 * SEQ).transpose(1, 0, 2) / SEQ ** 0.5
    over_g = np.concatenate([np.kron(np.eye(2), np.cos(g)), -np.kron(np.eye(2), np.sin(g))], axis=1) / FG ** 0.5
    dft = np.concatenate([over_t.reshape(P, -1), over_g], axis=1).astype(f32)
    swap = np.arange(HD).reshape(2, 2, 16)[:, ::-1].reshape(-1)
    gains = np.concatenate([a["e_q_gain"][0], a["e_q_gain"][0][swap], a["e_k_gain"][0], a["e_k_gain"][0][swap]])[None]

    arrays = {
        "stream": stream, "x_in": a["x"][0], "ctx_in": a["ctx"][0], "vecs": vecs, "consts": consts,
        "rope": rope, "dft": dft, "gains": gains, "ada_b": a["ada_b"], "norm_w": a["norm_w"].reshape(8, D),
        "late": late,
    }
    arrays = {k: np.ascontiguousarray(v) for k, v in arrays.items()}
    nc = bacc.Bacc("TRN2", target_bir_lowering=False, num_devices=1)
    args = [nc.dram_tensor(k, v.shape, F32, kind="ExternalInput").ap() for k, v in arrays.items()]
    out = nc.dram_tensor("out", (SEQ, D), F32, kind="ExternalOutput").ap()
    build(nc, *args, out)
    r = run_bass_kernel_spmd(nc, [arrays], core_ids=[0])
    return r.results[0]["out"].reshape(1, SEQ, D)
```

```python
from contextlib import ExitStack

import numpy as np

import concourse.bass as bass
from concourse import mybir

P = 128
D = 1024
KD = D // P
SEQ = 256
TB = SEQ // P
CTX = 256
NKB = (SEQ + CTX) // P
HD = 64
NQ, NKV = 12, 4
PAIRS = NQ // 2
AW, KW, FW = NQ * HD, NKV * HD, 256
FG = 64
GRID_W = 64
D_FF = 2816
NF = D_FF // P
E = 8
DE = 3584
NFE = DE // P
EPS = 1e-6
SCALE = HD ** -0.5
RING = 7
UNIT = 4096
BANK = 512
WIDTHS = (64, 96, 128, 144, 160, 192, 256)
WIDE = 2
BLOCKS = {64: [(0, 64)], 96: [(0, 64), (64, 32)], 128: [(0, 128)], 144: [(0, 128), (128, 32)],
          160: [(0, 128), (128, 32)],
          192: [(0, 128), (128, 64)], 256: [(0, 128), (128, 128)]}
HEAD_ORDER = [h for g in range(2) for i in range(3) for h in (6 * g + i, 6 * g + 3 + i)]

F32 = mybir.dt.float32
I32 = mybir.dt.int32
ALU = mybir.AluOpType
ACT = mybir.ActivationFunctionType
AX = mybir.AxisListType.X


ADA1_FROM = 3


def stream_order():
    order = [("mod", j) for j in range(4)] + [("win", j) for j in range(3)]
    ada0 = [("ada0", s, h) for s in range(4) for h in range(2)]
    ada1 = [("ada1", s, h) for s in range(6) for h in range(2)]
    order += ada0[:6] + [("wout", j) for j in range(2)] + ada0[6:]
    for u in range(NF // 2):
        order.append(("gu", u))
        if u >= ADA1_FROM:
            order += ada1[u - ADA1_FROM:u - ADA1_FROM + 1] if u < ADA1_FROM + 6 else []
    order += [("down", j) for j in range(-(-NF // 4))]
    for j in range(6):
        order += [("owin", j), ada1[6 + j]]
    order += [("owout", j) for j in range(2)]
    return order


ORDER = stream_order()
AT = {what: n for n, what in enumerate(ORDER)}
BASE = len(ORDER)
GU_UNITS = NFE // 2
PER_EXPERT = GU_UNITS + NFE // 4
UNITS = BASE + E * PER_EXPERT
assert PER_EXPERT % RING == 0
LAPS = PER_EXPERT // RING

V_C, V_B0, V_G, V_CONV, V_ROUTER, V_END = 0, 16, 32, 64, 88, 152
C_ID, C_ONE, C_REV, C_PICK, C_ROWS, C_END = 0, 128, 256, 264, 266, 270


def build(nc, stream, x_in, ctx_in, vecs, consts, rope, dft, gains, ada_b, norm_w, late, out):
    ctx = ExitStack()
    with ctx:
        def sb(name, shape, dt=F32):
            return ctx.enter_context(nc.sbuf_tensor(name, shape, dt))

        def sem(name):
            return ctx.enter_context(nc.semaphore(name))

        ring = sb("ring", [P, RING, UNIT])
        x = sb("x", [P, TB, D])
        hT = sb("hT", [P, KD, SEQ])
        xn = sb("xn", [P, TB, D])
        aT = sb("aT", [P, NFE * SEQ])
        hTe = sb("hTe", [P, KD, SEQ])
        acc = sb("acc", [P, 6 * D])
        gg = sb("gg", [P, 2, D])
        vec = sb("vec", [P, V_END])
        cst = sb("cst", [P, C_END])
        silu_c = sb("silu_c", [P, KD, 2])
        ab = sb("ab", [P, 5, 2, KD])
        mods0 = sb("mods0", [P, 2, KD, 2])
        stat = sb("stat", [P, 128])
        eps = sb("eps", [P, 1])
        width_at = sb("width_at", [1, E + 1], I32)
        ps = ctx.enter_context(nc.psum_tensor("ps", [P, 8, BANK], F32))

        ident, ones, rev = cst[:, C_ID:C_ID + P], cst[:, C_ONE:C_ONE + P], cst[:, C_REV:C_REV + E]
        pick, pick_rows = cst[:, C_PICK:C_PICK + 2], cst[:, C_ROWS:C_ROWS + 4]
        ctx_x = hTe[:, :, :].rearrange("p k t -> p (k t)").rearrange("p (b d) -> p b d", b=TB)
        hTc = acc[:, 4096:6144].rearrange("p (k t) -> p k t", k=KD)
        kz = acc[:, 4096:6144].rearrange("p (j t) -> p j t", j=NKV)
        mod_part = xn[:, :, :].rearrange("p b (h n) -> p (b h) n", h=2)
        qT = hTe[:, 0:PAIRS, :]
        mixT = hT
        q_tok = aT[:, 0:1536].rearrange("p (b n) -> p b n", b=TB)
        k_tok = aT[:, 1536:2560].rearrange("p (b n) -> p b n", b=NKB)
        probs = aT[:, 0:2048].rearrange("p (r n) -> p r n", r=4)
        probsT = aT[:, 3584:5632].rearrange("p (r n) -> p r n", r=4)
        v_tok = aT[:, 2560:3584].rearrange("p (b n) -> p b n", b=NKB)
        f_tok = aT[:, 3584:4096].rearrange("p (b n) -> p b n", b=TB)
        dftL = aT[:, 4096:5120].rearrange("p (b n) -> p b n", b=TB)
        dftD = aT[:, 5120:5376].rearrange("p (b n) -> p b n", b=2)
        roped = aT[:, 5376:5888]
        rope_t = aT[:, 5888:6400].rearrange("p (w c b n) -> p w c b n", w=2, c=2, b=TB)
        gain_t = aT[:, 6400:6656].rearrange("p (w c n) -> p w c n", w=2, c=2)
        rotated = aT[:, 6656:7168]
        fA = [roped, rotated]
        red_rows = rotated
        gated = hTe[:, 0:4, :]
        gated_e = hT[:, 0:4, :].rearrange("p (r k) t -> p r k t", r=2)
        aT_e = aT[:, :].rearrange("p (u b n) -> p u b n", b=2, n=256)
        conv_in = hTe[:, :, :].rearrange("p k t -> p (k t)")[:, 0:2 * (SEQ + 2)].rearrange("p (r n) -> p r n", r=2)
        conv_c = hTe[:, 4:6, :]
        conv_s = hTe[:, 6:8, :]
        y_sum = acc[:, 0:2048].rearrange("p (b d) -> p b d", b=TB)
        y_slot = acc[:, 2048:4096].rearrange("p (b d) -> p b d", b=2)
        sel = acc[:, 4096:4608].rearrange("p (b s) -> p b s", b=TB)
        selw = acc[:, 4608:5120].rearrange("p (b s) -> p b s", b=TB)
        selT = acc[:, 5120:5632].rearrange("p (b t) -> p b t", b=2)
        iota, before = acc[:, 5632:5888], acc[:, 5888:6016]

        def small(a, n, w):
            return acc[:, 6016 + a:6016 + a + 2 * n].rearrange("p (b e) -> p b e", b=TB)[:, :, 0:w]

        logit, tmp8, first, second, chosen = (small(16 * i, 8, 8) for i in range(5))
        slot_of, weight_of = small(80, 9, 9), small(98, 9, 9)

        landed = [sem(f"landed{s}") for s in range(RING)]
        used = [sem(f"used{s}") for s in range(RING)]
        small_in, x_in_s, ctx_in_s, tables_in = sem("small_in"), sem("x_in"), sem("ctx_in"), sem("tables_in")
        rows_in, bias_in, late_in = sem("rows_in"), sem("bias_in"), sem("late_in")
        acc_zero, tables_ok, psum_zero, eps_ok = sem("acc_zero"), sem("tables_ok"), sem("psum_zero"), sem("eps_ok")
        silu_ok, mod_sums, mod_ok = sem("silu_ok"), sem("mod_sums"), sem("mod_ok")
        dchain, achain, pchain = sem("dve_chain"), sem("act_chain"), sem("pool_chain")
        root, xn_ok, xT_ok, x_ok = sem("root"), sem("xn_ok"), sem("xT_ok"), sem("x_ok")
        hT_act, hT_dve, raw_act, raw_dve = sem("hT_act"), sem("hT_dve"), sem("raw_act"), sem("raw_dve")
        proj, square, ssum, qk_root = sem("proj"), sem("square"), sem("ssum"), sem("qk_root")
        head_ok, v_ok = sem("head_ok"), sem("v_ok")
        kT_ps, kT_ok, fA_ps, fA_ok, qT_ps, qT_ok, f_ps, f_ok = (
            sem(n) for n in ("kT_ps", "kT_ok", "fA_ps", "fA_ok", "qT_ps", "qT_ok", "f_ps", "f_ok"))
        score, negmax, prob, probT_ps, probT_ok, pv, o_ok = (
            sem(n) for n in ("score", "negmax", "prob", "probT_ps", "probT_ok", "pv", "o_ok"))
        y_ps, kz_zero, norm_p, mod_rows, mod_part_ok = (
            sem(n) for n in ("y_ps", "kz_zero", "norm_p", "mod_rows", "mod_part_ok"))
        red_ps, red_ok, rows_ok, ada_acc = sem("red_ps"), sem("red_ok"), sem("rows_ok"), sem("ada_acc")
        gu_ps, silu_out, a_ok = sem("gu_ps"), sem("silu_out"), sem("a_ok")
        c_out, z_ok, conv_ps = sem("c_out"), sem("z_ok"), sem("conv_ps")
        logit_ps, exp_in, exp_out, chosen_ok, rank_ps, width_ok = (
            sem(n) for n in ("logit_ps", "exp_in", "exp_out", "chosen_ok", "rank_ps", "width_ok"))
        sel_ok, selw_ok, gather_ps, hTe_act, hTe_dve = (
            sem(n) for n in ("sel_ok", "selw_ok", "gather_ps", "hTe_act", "hTe_dve"))
        e_ps, e_silu, e_a, eT_ps, eT_ok, selT_ps, selT_ok, ye_ps, ye_act, ye_dve, comb_ps, comb_ok = (
            sem(n) for n in ("e_ps", "e_silu", "e_a", "eT_ps", "eT_ok", "selT_ps", "selT_ok", "ye_ps", "ye_act", "ye_dve",
                             "comb_ps", "comb_ok"))
        stored = sem("stored")

        def slot(what):
            return ring[:, AT[what] % RING, :]

        def wait_landed(eng, what):
            n = AT[what]
            eng.wait_ge(landed[n % RING], 16 * (n // RING + 1))

        def used_up(ins, what):
            ins.then_inc(used[AT[what] % RING], 1)

        def pre_stat(norm, b):
            c = 4 * (TB * norm + b)
            return stat[:, c:c + 1], stat[:, c + 1:c + 2], stat[:, c + 2:c + 3]

        def post_stat(norm, b):
            c = 40 + 3 * (TB * norm + b)
            return stat[:, c:c + 1], stat[:, c + 1:c + 2], stat[:, c + 2:c + 3]

        HEADS = [4, 4, 4, 4, 8, 8, 4, 4]
        hstat = sb("hstat", [P, 3, 40])
        att = sb("att", [P, 3, TB * NQ])
        rt = sb("rt", [P, 8, TB])

        def hcols(i, blk):
            c = sum(HEADS[:blk])
            return hstat[:, i, c:c + HEADS[blk]]

        def y_bank(b):
            return ps[:, 4 + 2 * b:6 + 2 * b, :]

        block = ctx.enter_context(nc.Block())

        @block.sync
        def _(sp):
            sp.dma_start(vec[:, :], vecs).then_inc(small_in, 16)
            sp.dma_start(cst[:, :], consts).then_inc(small_in, 16)
            sp.dma_start(x[:, :, :], x_in.rearrange("(b p) d -> p b d", p=P)).then_inc(x_in_s, 16)
            sp.dma_start(ctx_x, ctx_in.rearrange("(b p) d -> p b d", p=P)).then_inc(ctx_in_s, 16)
            for s in range(RING):
                sp.dma_start(ring[:, s, :], stream[s, :, :]).then_inc(landed[s], 16)
            with sp.Fori(1, UNITS // RING) as lap:
                for s in range(RING):
                    sp.wait_ge(used[s], lap)
                    sp.dma_start(ring[:, s, :], stream[lap * RING + s, :, :]).then_inc(landed[s], 16)
            for s in range(UNITS % RING):
                sp.wait_ge(used[s], UNITS // RING)
                sp.dma_start(ring[:, s, :], stream[UNITS - UNITS % RING + s, :, :]).then_inc(landed[s], 16)

        @block.gpsimd
        def _(pool):
            pool.memset(acc[:, 0:4096], 0.0).then_inc(pchain, 1)
            pool.dma_start(dftL, dft[:, 0:1024].rearrange("p (b n) -> p b n", b=TB)).then_inc(tables_in, 16)
            pool.dma_start(dftD, dft[:, 1024:1280].rearrange("p (b n) -> p b n", b=2)).then_inc(tables_in, 16)
            pool.dma_start(rope_t.rearrange("p w c b n -> p (w c b n)"), rope).then_inc(tables_in, 16)
            pool.dma_start(gain_t.rearrange("p w c n -> p (w c n)"), gains.to_broadcast([P, 256])).then_inc(tables_in, 16)
            pool.wait_ge(pchain, 1)
            pool.dma_start(acc[0:1, 0:4096], ada_b[0:1, 2048:6144]).then_inc(bias_in, 16)
            for i in range(2):
                pool.dma_start(gg[:, i, :], norm_w[2 * i + 1:2 * i + 2, :].to_broadcast([P, D])).then_inc(rows_in, 16)
            pool.wait_ge(proj, 4)
            pool.memset(kz, 0.0).then_inc(kz_zero, 1)
            pool.wait_ge(red_ps, 6)
            pool.wait_ge(score, TB * NQ)
            pool.wait_ge(f_ps, 1)
            pool.memset(acc[:, :], 0.0).then_inc(pchain, 1)
            pool.wait_ge(pchain, 2)
            pool.dma_start(acc[0:1, :], ada_b[1:2, :]).then_inc(bias_in, 16)
            pool.wait_ge(x_ok, 2 * TB)
            for i in range(2):
                pool.dma_start(gg[:, i, :], norm_w[4 + 2 * i + 1:4 + 2 * i + 2, :].to_broadcast([P, D])).then_inc(rows_in, 16)
            pool.wait_ge(red_ps, 13)
            pool.dma_start(acc[:, 5632:6016], late).then_inc(late_in, 16)

        @block.scalar
        def _(act):
            links = [0]

            def link(ins):
                links[0] += 1
                ins.then_inc(achain, 1)
                act.wait_ge(achain, links[0])

            def rms(src, junk, st, n):
                link(act.activation(junk, src, ACT.Square, accum_out=st[0]))
                act.activation(st[1], st[0], ACT.Sqrt, bias=eps[:, 0:1], scale=1.0 / n).then_inc(root, 1)

            act.wait_ge(small_in, 32)
            act.activation(silu_c[:, :, :], vec[:, V_C:V_C + 2 * KD].rearrange("p (k v) -> p k v", v=2),
                           ACT.Silu).then_inc(silu_ok, 1)
            act.wait_ge(eps_ok, 1)
            act.wait_ge(x_in_s, 16)
            for b in range(TB):
                rms(x[:, b, :], xn[:, b, :], pre_stat(0, b), D)
            act.wait_ge(ctx_in_s, 16)
            for b in range(TB):
                rms(ctx_x[:, b, :], acc[:, 4096 + D * b:4096 + D * (b + 1)], pre_stat(1, b), D)
            act.wait_ge(xT_ok, TB)
            for j in range(4):
                act.activation(hT[:, 2 * j:2 * j + 2, :].rearrange("p k t -> p (k t)"), ps[:, j, :],
                               ACT.Copy).then_inc(raw_act, 1)
            for j in range(4):
                act.wait_ge(mod_rows, j + 1)
                act.activation(mod_part[:, j, :], ps[:, j, :], ACT.Copy).then_inc(mod_part_ok, 1)
            act.wait_ge(mod_ok, 1)
            act.wait_ge(raw_dve, 4)
            for k in range(KD):
                act.activation(hTc[:, k, :], hTc[:, k, :], ACT.Identity, bias=ab[:, 1, 1, k:k + 1],
                               scale=ab[:, 1, 0, k:k + 1]).then_inc(hT_act, 1)
            for blk in range(8):
                nh = HEADS[blk]
                act.wait_ge(proj, blk + 1)
                if blk < NKB:
                    dst = k_tok[:, blk, :]
                else:
                    dst = q_tok[:, blk % 2, (0 if blk < 6 else 512):(512 if blk < 6 else 768)]
                act.activation(dst, ps[:, blk, 0:nh * HD], ACT.Square).then_inc(square, 1)
                if blk < NKB:
                    act.activation(v_tok[:, blk, :], ps[:, blk, 256:512], ACT.Copy).then_inc(v_ok, 1)
                elif blk >= 6:
                    act.activation(f_tok[:, blk % 2, :], ps[:, blk, 256:512], ACT.Copy).then_inc(v_ok, 1)
                act.wait_ge(ssum, blk + 1)
                act.activation(hcols(1, blk), hcols(0, blk), ACT.Sqrt, bias=eps[:, 0:1],
                               scale=1.0 / HD).then_inc(qk_root, 1)
            act.wait_ge(kz_zero, 1)
            act.wait_ge(kT_ps, 2)
            for j in range(2):
                for a in range(2):
                    rows = slice(a * HD, (a + 1) * HD)
                    act.activation(kz[rows, 2 * j + a, :], ps[rows, j, :], ACT.Copy).then_inc(kT_ok, 1)
            act.wait_ge(qT_ps, 1)
            for j in range(3):
                act.activation(qT[:, 2 * j:2 * j + 2, :].rearrange("p k t -> p (k t)"), ps[:, 4 + j, :],
                               ACT.Copy).then_inc(qT_ok, 1)
            for n in range(TB * NQ + 3):
                m = n - 3
                if m >= 0:
                    act.wait_ge(probT_ps, m + 1)
                    if m >= 4:
                        act.wait_ge(pv, (m - 4) // 2 + 1)
                    act.activation(probsT[:, m % 4, :], ps[:, 4 + m % 2, :], ACT.Copy).then_inc(probT_ok, 1)
                if n < TB * NQ:
                    act.wait_ge(negmax, n + 1)
                    if n >= 4:
                        act.wait_ge(probT_ps, n - 3)
                    act.activation(probs[:, n % 4, :], ps[:, n % 4, :], ACT.Exp, bias=att[:, 0, n:n + 1],
                                   accum_out=att[:, 1, n:n + 1]).then_inc(prob, 1)
                if n == 2:
                    act.wait_ge(f_ps, 1)
                    act.activation(mixT[:, 6:8, :].rearrange("p k t -> p (k t)"), ps[:, 7, :],
                                   ACT.Copy).then_inc(f_ok, 1)

            def post_pre(post, pre):
                for b in range(TB):
                    act.wait_ge(y_ps, TB * post + b + 1)
                    rms(y_bank(b).rearrange("p a n -> p (a n)"), xn[:, b, :], post_stat(post, b), D)
                    act.wait_ge(x_ok, TB * post + b + 1)
                    rms(x[:, b, :], xn[:, b, :], pre_stat(pre, b), D)
                    act.wait_ge(xT_ok, TB * pre + b + 1)
                    for k in range(KD // 2):
                        act.activation(hT[:, k, b * P:(b + 1) * P], ps[:, 4 + 2 * b, k * P:(k + 1) * P],
                                       ACT.Identity, bias=ab[:, pre, 1, k:k + 1],
                                       scale=ab[:, pre, 0, k:k + 1]).then_inc(hT_act, 1)

            post_pre(0, 2)
            for j in range(NF):
                act.wait_ge(gu_ps, j + 1)
                act.activation(gated[:, j % 4, :], ps[:, j % 4, 0:SEQ], ACT.Silu).then_inc(silu_out, 1)
            post_pre(1, 3)
            for j in range(KD):
                act.wait_ge(conv_ps, j + 1)
                if j >= 2:
                    act.wait_ge(z_ok, j - 1)
                act.activation(conv_c[:, j % 2, :], ps[:, 2 * (j % 2), SEQ:2 * SEQ], ACT.Copy).then_inc(c_out, 1)
            post_pre(2, 4)
            act.wait_ge(exp_in, 1)
            act.activation(rt[:, 4, :], rt[:, 3, :], ACT.Exp).then_inc(exp_out, 1)

            def take_gather(count):
                for k in range(KD // 2):
                    if k % 2 == 0:
                        act.wait_ge(gather_ps, count + k // 2 + 1)
                    act.activation(hTe[:, k, :], ps[:, k // 2, (k % 2) * SEQ:(k % 2 + 1) * SEQ], ACT.Identity,
                                   bias=ab[:, 4, 1, k:k + 1], scale=ab[:, 4, 0, k:k + 1]).then_inc(hTe_act, 1)

            take_gather(0)
            act.wait_ge(width_ok, 1)
            with act.Fori(0, E) as e:
                which = act.value_load(width_at[0:1, bass.ds(e, 1)], min_val=0, max_val=len(WIDTHS))

                def take_turned(u):
                    act.wait_ge(eT_ps, e * GU_UNITS + u + 1)
                    act.activation(aT_e[:, u, :, :].rearrange("p b n -> p (b n)"), ps[:, 6 + u % 2, :],
                                   ACT.Copy).then_inc(eT_ok, 1)

                def silu_units(wide):
                    for u in range(GU_UNITS):
                        act.wait_ge(e_ps, e * GU_UNITS + u + 1)
                        q = 2 * (u % 2)
                        act.activation(gated_e[:, u % 2, :, :], ps[:, q:q + 2, 0:SEQ], ACT.Silu).then_inc(e_silu, 1)
                        if u and not wide:
                            take_turned(u - 1)
                        if u == 5:
                            act.wait_ge(selT_ps, e + 1)
                            act.activation(selT[:, :, :].rearrange("p b t -> p (b t)"), ps[:, 4, :],
                                           ACT.Copy).then_inc(selT_ok, 1)
                    if wide:
                        act.sem_inc(eT_ok, GU_UNITS)
                    else:
                        take_turned(GU_UNITS - 1)

                with act.If(which < WIDE):
                    silu_units(False)
                with act.If(which >= WIDE):
                    silu_units(True)
                act.wait_ge(ye_ps, e + 1)
                for b in range(2):
                    act.activation(y_slot[:, b, 0:BANK], ps[:, 4 + 2 * b, :], ACT.Copy).then_inc(ye_act, 1)
                with act.If(e < E - 1):
                    take_gather(e * 4 + 4)
            act.activation(stat[:, 127:128], eps[:, 0:1], ACT.Sqrt)
            for b in range(TB):
                act.wait_ge(comb_ok, 4 * E + 2 * b + 2)
                rms(y_sum[:, b, :], xn[:, b, :], post_stat(3, b), D)
            for b in range(TB):
                act.wait_ge(x_ok, 3 * TB + b + 1)
                act.dma_start(out[b * P:(b + 1) * P, :], x[:, b, :]).then_inc(stored, 16)
            act.wait_ge(stored, 16 * TB)

        @block.vector
        def _(dve):
            links = [0]

            def link(ins):
                links[0] += 1
                ins.then_inc(dchain, 1)
                dve.wait_ge(dchain, links[0])

            dve.memset(eps[:, :], EPS).then_inc(eps_ok, 1)
            dve.memset(ps[:, :, :], 0.0).then_inc(psum_zero, 1)

            roots = [0]

            def norm_rows(src, dst, st):
                roots[0] += 1
                dve.wait_ge(root, roots[0])
                link(dve.reciprocal(st[2], st[1]))
                dve.tensor_scalar(dst, src, st[2], None, ALU.mult).then_inc(xn_ok, 1)

            dve.wait_ge(x_in_s, 16)
            for b in range(TB):
                norm_rows(x[:, b, :], xn[:, b, :], pre_stat(0, b))
            dve.wait_ge(ctx_in_s, 16)
            for b in range(TB):
                norm_rows(ctx_x[:, b, :], ctx_x[:, b, :], pre_stat(1, b))
            dve.wait_ge(xT_ok, 2 * TB)
            for j in range(4):
                dve.tensor_copy(hTc[:, 2 * j:2 * j + 2, :].rearrange("p k t -> p (k t)"),
                                ps[:, 4 + j, :]).then_inc(raw_dve, 1)
            dve.wait_ge(small_in, 32)
            dve.wait_ge(mod_sums, 1)
            b0 = vec[:, V_B0:V_B0 + 16]
            link(dve.tensor_tensor(mods0[:, :, :, :].rearrange("p s k v -> p (s k) v"),
                                   ps[:, 4, 0:32].rearrange("p (m v) -> p m v", v=2),
                                   b0.unsqueeze(2).to_broadcast([P, 16, 2]), ALU.add))
            for v in range(2):
                dve.tensor_copy(ab[:, v, 1, :], mods0[:, 0, :, v])
                last = dve.scalar_tensor_tensor(out=ab[:, v, 0, :], in0=mods0[:, 1, :, v], scalar=1.0,
                                                in1=vec[:, V_G:V_G + KD], op0=ALU.add, op1=ALU.mult)
            last.then_inc(mod_ok, 1)
            dve.wait_ge(mod_ok, 1)
            dve.wait_ge(raw_act, 4)
            for k in range(KD):
                dve.tensor_scalar(hT[:, k, :], hT[:, k, :], ab[:, 0, 0, k:k + 1], ab[:, 0, 1, k:k + 1],
                                  ALU.mult, ALU.add).then_inc(hT_dve, 1)

            def ada_unit(layer, s, h, parts=range(4), cols=slice(0, D)):
                what = (f"ada{layer}", s, h)
                if parts[0] == 0 and cols.start == 0:
                    if s == 0 and h == 0:
                        dve.wait_ge(bias_in, 16 * (layer + 1))
                    wait_landed(dve, what)
                dst = acc[:, s * D:(s + 1) * D][:, cols]
                for k in parts:
                    last = dve.scalar_tensor_tensor(out=dst, in0=slot(what)[:, k * D:(k + 1) * D][:, cols],
                                                    scalar=silu_c[:, 4 * h + k, 0:1], in1=dst,
                                                    op0=ALU.mult, op1=ALU.add)
                    if k < 3 or cols.stop < D:
                        link(last)
                if parts[-1] < 3 or cols.stop < D:
                    return
                used_up(last, what)
                n = AT[what]
                dve.wait_ge(used[n % RING], n // RING + 1)
                dve.sem_inc(ada_acc, 1)

            def head_block(blk):
                nh = HEADS[blk]
                w = 1 if blk < NKB else 0
                if blk < NKB:
                    dst = k_tok[:, blk, :]
                else:
                    dst = q_tok[:, blk % 2, (0 if blk < 6 else 512):(512 if blk < 6 else 768)]
                heads = dst.rearrange("p (h d) -> p h d", d=HD)
                dve.wait_ge(square, blk + 1)
                dve.tensor_reduce(hcols(0, blk), heads, AX, ALU.add).then_inc(ssum, 1)
                dve.wait_ge(qk_root, blk + 1)
                link(dve.reciprocal(hcols(2, blk), hcols(1, blk)))
                link(dve.tensor_tensor(heads, ps[:, blk, 0:nh * HD].rearrange("p (h d) -> p h d", d=HD),
                                       hcols(2, blk).unsqueeze(2).to_broadcast([P, nh, HD]), ALU.mult))
                if 2 <= blk < NKB:
                    dve.tensor_tensor(heads, heads, gain_t[:, 1, 0:1, :].to_broadcast([P, nh, HD]),
                                      ALU.mult).then_inc(head_ok, 1)
                    return
                b = blk % 2
                dve.tensor_tensor(roped[:, 0:nh * HD].rearrange("p (h d) -> p h d", d=HD), heads,
                                  rope_t[:, w, 0, b:b + 1, :].to_broadcast([P, nh, HD]), ALU.mult)
                for a in range(2):
                    part = dst.rearrange("p (h x a d) -> p h x a d", x=2, a=2, d=16)[:, :, :, 1 - a, :]
                    to = rotated[:, 0:nh * HD].rearrange("p (h x a d) -> p h x a d", x=2, a=2, d=16)[:, :, :, a, :]
                    tab = rope_t[:, w, 1, b, :].rearrange("p (x a d) -> p x a d", x=2, a=2)[:, :, a, :]
                    last = dve.tensor_tensor(to, part, tab.unsqueeze(1).to_broadcast([P, nh, 2, 16]), ALU.mult)
                link(last)
                dve.tensor_tensor(dst, roped[:, 0:nh * HD], rotated[:, 0:nh * HD], ALU.add).then_inc(head_ok, 1)
                dve.wait_ge(head_ok, blk + 1)

            dve.wait_ge(tables_in, 64)
            for w in range(2):
                for c in range(2):
                    last = dve.tensor_tensor(rope_t[:, w, c, :, :], rope_t[:, w, c, :, :],
                                             gain_t[:, w, c:c + 1, :].to_broadcast([P, TB, HD]), ALU.mult)
            link(last)

            head_block(0)
            for n, blks in enumerate([(1,), (2,), (3, 4, 5, 6, 7)]):
                ada_unit(0, n // 2, n % 2)
                for blk in blks:
                    head_block(blk)
            dve.wait_ge(fA_ps, 1)
            for j in range(2):
                dve.tensor_copy(fA[j], ps[:, 2 + j, :]).then_inc(fA_ok, 1)

            for n in range(TB * NQ + 6):
                if n < TB * NQ:
                    dve.wait_ge(score, n + 1)
                    dve.tensor_reduce(att[:, 0, n:n + 1], ps[:, n % 4, :], AX, ALU.max,
                                      negate=True).then_inc(negmax, 1)
                m = n - 1
                if 0 <= m < TB * NQ:
                    dve.wait_ge(prob, m + 1)
                    link(dve.reciprocal(att[:, 2, m:m + 1], att[:, 1, m:m + 1]))
                    dve.tensor_scalar(probs[:, m % 4, :], probs[:, m % 4, :], att[:, 2, m:m + 1], None,
                                      ALU.mult).then_inc(norm_p, 1)
                if n < TB * NQ:
                    unit, half, k = 3 + n // 8, (n // 4) % 2, n % 4
                    ada_unit(0, unit // 2, unit % 2, [k], slice(half * BANK, (half + 1) * BANK))
                m = n - 6
                if m >= 0 and m % 2:
                    i, b = m // 4, (m // 2) % 2
                    dve.wait_ge(pv, m // 2 + 1)
                    dve.tensor_copy(mixT[:, i, b * P:(b + 1) * P], ps[:, 6 + b, 0:P]).then_inc(o_ok, 1)

            def gate_half(i, bank):
                half = gg[:, i // 2, (i % 2) * BANK:(i % 2 + 1) * BANK]
                dve.tensor_tensor(half, half, ps[:, bank, :], ALU.mult).then_inc(red_ok, 1)

            def rows_out(bank):
                dve.tensor_copy(red_rows, ps[:, bank, :]).then_inc(rows_ok, 1)

            def factors(pre, bank, g):
                def blocks(a):
                    return a.rearrange("p (r m) -> p r m", m=4)

                src = ps[:, bank, 0:16].rearrange("p (m r) -> p r m", r=4)
                dve.tensor_copy(blocks(ab[:, pre, 1, :]), src[:, 0:2, :])
                dve.scalar_tensor_tensor(out=blocks(ab[:, pre, 0, :]), in0=src[:, 2:4, :], scalar=1.0,
                                         in1=blocks(vec[:, V_G + KD * g:V_G + KD * (g + 1)]), op0=ALU.add,
                                         op1=ALU.mult).then_inc(red_ok, 1)

            dve.wait_ge(rows_in, 32)
            for i in range(2):
                dve.wait_ge(red_ps, i + 1)
                gate_half(i, i)
            dve.wait_ge(red_ps, 3)
            rows_out(2)
            ada_unit(0, 3, 0)
            ada_unit(0, 3, 1)
            dve.wait_ge(red_ps, 4)
            factors(2, 2, 1)

            def post_pre(post, pre):
                for b in range(TB):
                    st = post_stat(post, b)
                    roots[0] += 1
                    dve.wait_ge(root, roots[0])
                    link(dve.reciprocal(st[2], st[1]))
                    link(dve.scalar_tensor_tensor(out=xn[:, b, :], in0=y_bank(b).rearrange("p a n -> p (a n)"),
                                                  scalar=st[2], in1=gg[:, post % 2, :], op0=ALU.mult, op1=ALU.mult))
                    dve.tensor_tensor(x[:, b, :], x[:, b, :], xn[:, b, :], ALU.add).then_inc(x_ok, 1)
                    norm_rows(x[:, b, :], xn[:, b, :], pre_stat(pre, b))
                    dve.wait_ge(xT_ok, TB * pre + b + 1)
                    for k in range(KD // 2, KD):
                        dve.tensor_scalar(hT[:, k, b * P:(b + 1) * P], ps[:, 5 + 2 * b, (k % 4) * P:(k % 4 + 1) * P],
                                          ab[:, pre, 0, k:k + 1], ab[:, pre, 1, k:k + 1], ALU.mult,
                                          ALU.add).then_inc(hT_dve, 1)

            post_pre(0, 2)
            units1 = [(s, h) for s in range(6) for h in range(2)]
            for j in range(NF):
                dve.wait_ge(silu_out, j + 1)
                dve.tensor_tensor(aT[:, j * SEQ:(j + 1) * SEQ], gated[:, j % 4, :], ps[:, j % 4, SEQ:2 * SEQ],
                                  ALU.mult).then_inc(a_ok, 1)
                if j == 3:
                    for i in range(2):
                        dve.wait_ge(red_ps, 5 + i)
                        gate_half(2 + i, 4 + i)
                if j % 2 and ADA1_FROM <= j // 2 < ADA1_FROM + 6:
                    ada_unit(1, *units1[j // 2 - ADA1_FROM])
            dve.wait_ge(red_ps, 7)
            rows_out(7)
            dve.wait_ge(red_ps, 8)
            factors(3, 0, 2)
            post_pre(1, 3)
            link(dve.memset(conv_in, 0.0))
            for j in range(KD):
                r = j % 2
                dve.wait_ge(c_out, j + 1)
                link(dve.tensor_tensor(conv_in[:, r, 1:SEQ + 1], conv_c[:, r, :], ps[:, 2 * r + 1, 0:SEQ], ALU.mult))
                link(dve.tensor_scalar(conv_s[:, r, :], conv_in[:, r, 0:SEQ], vec[:, V_CONV + j:V_CONV + j + 1],
                                       None, ALU.mult))
                for t in (1, 2):
                    c = V_CONV + KD * t + j
                    link(dve.scalar_tensor_tensor(out=conv_s[:, r, :], in0=conv_in[:, r, t:t + SEQ],
                                                  scalar=vec[:, c:c + 1], in1=conv_s[:, r, :], op0=ALU.mult,
                                                  op1=ALU.add))
                dve.tensor_tensor(aT[:, j * SEQ:(j + 1) * SEQ], conv_s[:, r, :], ps[:, 2 * r, 0:SEQ],
                                  ALU.mult).then_inc(z_ok, 1)
                if 1 <= j < 7:
                    ada_unit(1, *units1[5 + j])
            dve.wait_ge(red_ps, 9)
            rows_out(7)
            dve.wait_ge(rows_in, 64)
            for i in range(4):
                dve.wait_ge(red_ps, 10 + i)
                gate_half(i, i)
            for i in range(4):
                dve.memset(y_sum[:, i // 2, (i % 2) * BANK:(i % 2 + 1) * BANK], 0.0).then_inc(comb_ok, 1)
            dve.wait_ge(red_ps, 14)
            factors(4, 0, 3)
            post_pre(2, 4)

            dve.wait_ge(late_in, 16)

            def rb(i):
                return rt[:, i, :].unsqueeze(2).to_broadcast([P, TB, E])

            revb = rev.unsqueeze(1).to_broadcast([P, TB, E])
            dve.wait_ge(logit_ps, 1)
            link(dve.tensor_copy(logit, ps[:, 0, 0:TB * E].rearrange("p (b e) -> p b e", b=TB)))

            def top(values, mask, i):
                link(dve.tensor_reduce(rt[:, i, :], values, AX, ALU.max))
                link(dve.tensor_tensor(mask, values, rb(i), ALU.is_equal))
                link(dve.tensor_tensor(mask, mask, revb, ALU.mult))
                link(dve.tensor_reduce(rt[:, 2, :], mask, AX, ALU.max))
                link(dve.tensor_tensor(mask, revb, rb(2), ALU.is_equal))

            top(logit, first, 0)
            link(dve.scalar_tensor_tensor(out=tmp8, in0=first, scalar=-3.0e38, in1=logit, op0=ALU.mult, op1=ALU.add))
            top(tmp8, second, 1)
            dve.tensor_tensor(chosen, first, second, ALU.add).then_inc(chosen_ok, 1)
            dve.tensor_tensor(rt[:, 3, :], rt[:, 1, :], rt[:, 0, :], ALU.subtract).then_inc(exp_in, 1)
            dve.wait_ge(exp_out, 1)
            link(dve.tensor_scalar(rt[:, 5, :], rt[:, 4, :], 1.0, None, ALU.add))
            link(dve.reciprocal(rt[:, 6, :], rt[:, 5, :]))
            link(dve.tensor_tensor(rt[:, 7, :], rt[:, 4, :], rt[:, 6, :], ALU.mult))
            link(dve.tensor_tensor(first, first, rb(6), ALU.mult))
            link(dve.tensor_tensor(second, second, rb(7), ALU.mult))
            link(dve.memset(weight_of, 0.0))
            link(dve.memset(slot_of, -1.0))
            link(dve.tensor_tensor(weight_of[:, :, 0:E], first, second, ALU.add))
            dve.wait_ge(rank_ps, 1)
            link(dve.scalar_tensor_tensor(out=slot_of[:, :, 0:E], in0=ps[:, 1, 0:TB * E].rearrange("p (b e) -> p b e", b=TB),
                                          scalar=1.0, in1=chosen, op0=ALU.add, op1=ALU.mult))
            link(dve.tensor_scalar(slot_of[:, :, 0:E], slot_of[:, :, 0:E], -1.0, None, ALU.add))
            count = ps[0:1, 2, 0:E]
            wsum = hstat[0:1, 0, 0:E]
            link(dve.tensor_scalar(wsum, count, float(WIDTHS[0]), None, ALU.is_gt))
            for w in WIDTHS[1:-1]:
                link(dve.scalar_tensor_tensor(out=wsum, in0=count, scalar=float(w), in1=wsum, op0=ALU.is_gt, op1=ALU.add))
            link(dve.memset(width_at[:, :], len(WIDTHS)))
            dve.tensor_copy(width_at[0:1, 0:E], wsum).then_inc(width_ok, 1)

            def select(e, weighted):
                for b in range(TB):
                    at = slot_of[:, b, bass.ds(e, 1)]
                    if weighted:
                        last = dve.tensor_scalar(selw[:, b, :], iota, at, weight_of[:, b, bass.ds(e, 1)],
                                                 ALU.is_equal, ALU.mult)
                    else:
                        last = dve.tensor_scalar(sel[:, b, :], iota, at, None, ALU.is_equal)
                last.then_inc(selw_ok if weighted else sel_ok, 1)

            def take_gather(count):
                for k in range(KD // 2, KD):
                    if k % 2 == 0:
                        dve.wait_ge(gather_ps, count + k // 2 + 1)
                    dve.tensor_scalar(hTe[:, k, :], ps[:, k // 2, (k % 2) * SEQ:(k % 2 + 1) * SEQ],
                                      ab[:, 4, 0, k:k + 1], ab[:, 4, 1, k:k + 1], ALU.mult,
                                      ALU.add).then_inc(hTe_dve, 1)

            select(0, False)
            select(0, True)
            take_gather(0)
            with dve.Fori(0, E) as e:
                dve.wait_ge(gather_ps, e * 4 + 4)
                select(e + 1, False)
                for u in range(GU_UNITS):
                    dve.wait_ge(e_silu, e * GU_UNITS + u + 1)
                    q = 2 * (u % 2)
                    dve.tensor_tensor(aT_e[:, u, :, :], gated_e[:, u % 2, :, :], ps[:, q:q + 2, SEQ:2 * SEQ],
                                      ALU.mult).then_inc(e_a, 1)
                    if u == 7:
                        dve.wait_ge(selT_ps, e + 1)
                        select(e + 1, True)
                dve.wait_ge(ye_ps, e + 1)
                for b in range(2):
                    dve.tensor_copy(y_slot[:, b, BANK:2 * BANK], ps[:, 5 + 2 * b, :]).then_inc(ye_dve, 1)
                with dve.If(e < E - 1):
                    take_gather(e * 4 + 4)
                for i in range(4):
                    dve.wait_ge(comb_ps, e * 4 + i + 1)
                    part = y_sum[:, i // 2, (i % 2) * BANK:(i % 2 + 1) * BANK]
                    dve.tensor_tensor(part, part, ps[:, 4 + i, :], ALU.add).then_inc(comb_ok, 1)
            for b in range(TB):
                st = post_stat(3, b)
                roots[0] += 1
                dve.wait_ge(root, roots[0])
                link(dve.reciprocal(st[2], st[1]))
                link(dve.scalar_tensor_tensor(out=xn[:, b, :], in0=y_sum[:, b, :], scalar=st[2],
                                              in1=gg[:, 1, :], op0=ALU.mult, op1=ALU.mult))
                dve.tensor_tensor(x[:, b, :], x[:, b, :], xn[:, b, :], ALU.add).then_inc(x_ok, 1)

        @block.tensor
        def _(pe):
            def turn_rows(src, bank0, order):
                for b in range(TB):
                    pe.wait_ge(xn_ok, order * TB + b + 1)
                    for k in range(KD):
                        last = pe.transpose(ps[:, bank0 + k // 2, (k % 2) * SEQ + b * P:(k % 2) * SEQ + (b + 1) * P],
                                            src[:, b, k * P:(k + 1) * P], ident)
                    last.then_inc(xT_ok, 1)

            pe.wait_ge(small_in, 32)
            pe.wait_ge(psum_zero, 1)
            turn_rows(xn, 0, 0)
            turn_rows(ctx_x, 4, 1)
            pe.wait_ge(silu_ok, 1)
            pe.wait_ge(raw_act, 4)
            pe.wait_ge(raw_dve, 1)

            def mod_columns(j):
                pe.wait_ge(mod_part_ok, j + 1)
                for m in range(4):
                    c = 2 * (4 * j + m)
                    last = pe.matmul(ps[:, 4, c:c + 2], mod_part[:, j, m * P:(m + 1) * P], pick,
                                     start=True, stop=True)
                return last

            for j in range(4):
                wait_landed(pe, ("mod", j))
                w = slot(("mod", j)).rearrange("p (k n) -> p k n", k=KD)
                for half in range(2):
                    for r in range(4):
                        last = pe.matmul(ps[32 * r:32 * r + 2, j, :], silu_c[:, 2 * r + half, :],
                                         w[:, 2 * r + half, :], start=(half == 0), stop=(half == 1))
                last.then_inc(mod_rows, 1)
                if j:
                    used_up(mod_columns(j - 1), ("mod", j - 1))
            mod_columns(3).then_inc(mod_sums, 1)
            for blk in range(8):
                unit = ("win", 0 if blk < 4 else 1 if blk < 6 else 2)
                lhs = hTc if blk in (2, 3) else hT
                b = blk % 2
                wait_landed(pe, unit)
                w = slot(unit).rearrange("p (k n) -> p k n", k=KD)
                if blk == 0:
                    pe.wait_ge(mod_part_ok, 4)
                if blk == 4:
                    pe.wait_ge(raw_dve, 4)
                for k in range(KD):
                    if blk == 0:
                        pe.wait_ge(hT_dve, k + 1)
                    if blk == 2:
                        pe.wait_ge(hT_act, k + 1)
                    last = pe.matmul(ps[:, blk, :], lhs[:, k, b * P:(b + 1) * P], w[:, k, :],
                                     start=(k == 0), stop=(k == KD - 1))
                    if k == 0 and blk in (0, 4, 6):
                        used_up(last, {0: ("mod", 3), 4: ("win", 0), 6: ("win", 1)}[blk])
                last.then_inc(proj, 1)
            pe.wait_ge(head_ok, 4)
            pe.wait_ge(v_ok, 4)
            for j in range(2):
                for b in range(NKB):
                    last = pe.transpose(ps[:, j, b * P:(b + 1) * P], k_tok[:, b, j * P:(j + 1) * P], ident)
                    if j == 0 and b == 0:
                        used_up(last, ("win", 2))
                last.then_inc(kT_ps, 1)
            pe.wait_ge(v_ok, 6)
            pe.wait_ge(tables_in, 64)
            for j in range(2):
                for b in range(TB):
                    last = pe.matmul(ps[:, 2 + j, :], f_tok[:, b, j * P:(j + 1) * P], dftL[:, b, :],
                                     start=(b == 0), stop=(b == TB - 1))
            last.then_inc(fA_ps, 1)
            pe.wait_ge(head_ok, 8)
            for i in range(PAIRS):
                for b in range(TB):
                    last = pe.transpose(ps[:, 4 + i // 2, (i % 2) * SEQ + b * P:(i % 2) * SEQ + (b + 1) * P],
                                        q_tok[:, b, i * P:(i + 1) * P], ident)
            last.then_inc(qT_ps, 1)
            pe.wait_ge(kT_ok, 4)
            pe.wait_ge(qT_ok, 3)
            pe.wait_ge(fA_ok, 2)
            for n in range(TB * NQ + 5):
                if n < TB * NQ:
                    i, b, a = n // 4, (n // 2) % 2, n % 2
                    if n >= 4:
                        pe.wait_ge(prob, n - 3)
                    pe.matmul(ps[:, n % 4, :], qT[:, i, b * P:(b + 1) * P], kz[:, 2 * (i // 3) + a, :],
                              start=True, stop=True).then_inc(score, 1)
                if n == 2:
                    for j in range(2):
                        for c in range(2):
                            last = pe.matmul(ps[:, 7, j * SEQ:(j + 1) * SEQ], dftD[:, c, :],
                                             fA[j][:, c * SEQ:(c + 1) * SEQ], start=(c == 0), stop=(c == 1))
                    last.then_inc(f_ps, 1)
                m = n - 3
                if 0 <= m < TB * NQ:
                    pe.wait_ge(norm_p, m + 1)
                    if m >= 2:
                        pe.wait_ge(probT_ok, m - 1)
                    for b in range(NKB):
                        last = pe.transpose(ps[:, 4 + m % 2, b * P:(b + 1) * P],
                                            probs[:, m % 4, b * P:(b + 1) * P], ident)
                    last.then_inc(probT_ps, 1)
                m = n - 5
                if m >= 0 and m % 2:
                    i, b = m // 4, (m // 2) % 2
                    pe.wait_ge(probT_ok, m + 1)
                    if m == 3:
                        pe.wait_ge(f_ok, 1)
                    if m >= 5:
                        pe.wait_ge(o_ok, m // 2 - 1)
                    for kb in range(NKB):
                        for a in range(2):
                            kv = 2 * (i // 3) + a
                            last = pe.matmul(ps[a * HD:(a + 1) * HD, 6 + b, 0:P], v_tok[:, kb, kv * HD:(kv + 1) * HD],
                                             probsT[:, (m - 1 + a) % 4, kb * P:(kb + 1) * P],
                                             start=(kb == 0), stop=(kb == NKB - 1))
                    last.then_inc(pv, 1)
            pe.wait_ge(ada_acc, 6)
            pe.wait_ge(prob, TB * NQ)
            for i in range(2):
                pe.matmul(ps[:, i, :], ones, acc[:, i * BANK:(i + 1) * BANK], start=True, stop=True).then_inc(red_ps, 1)

            def sum_rows(c, bank, before=None):
                for r in range(4):
                    last = pe.matmul(ps[32 * r:32 * (r + 1), bank, :], ones[:, 0:32],
                                     acc[:, c + r * BANK:c + (r + 1) * BANK], start=True, stop=True)
                    if r == 0 and before:
                        used_up(last, before)
                last.then_inc(red_ps, 1)

            def columns(bank):
                for m in range(4):
                    last = pe.matmul(ps[:, bank, 4 * m:4 * m + 4], red_rows[:, m * P:(m + 1) * P], pick_rows,
                                     start=True, stop=True)
                last.then_inc(red_ps, 1)

            sum_rows(D, 2)

            def turn(pre, b, before=None):
                pe.wait_ge(xn_ok, TB * pre + b + 1)
                for k in range(KD):
                    last = pe.transpose(ps[:, 4 + 2 * b + k // 4, (k % 4) * P:(k % 4 + 1) * P],
                                        xn[:, b, k * P:(k + 1) * P], ident)
                    if k == 0 and before:
                        used_up(last, before)
                last.then_inc(xT_ok, 1)

            def wait_hT(pre, b, k):
                half = KD // 2
                pe.wait_ge(hT_act if k < half else hT_dve, KD + KD * (pre - 2) + half * b + k % half + 1)

            def project(units, per_unit, nblocks, lhs, pre, inserted, lhs_ok=None):
                for b in range(TB):
                    for k in range(nblocks):
                        unit = units[k // per_unit]
                        if b == 0 and k % per_unit == 0:
                            wait_landed(pe, unit)
                        w = slot(unit).rearrange("p (k n) -> p k n", k=per_unit)
                        if (b, k) in inserted:
                            inserted[b, k]()
                        if b == 0 and lhs_ok is not None:
                            pe.wait_ge(lhs_ok, k + 1)
                        if b == 1 and k == nblocks - 2:
                            turn(pre, 0)
                        for h in range(2):
                            last = pe.matmul(ps[:, 4 + 2 * b + h, :], lhs(k)[:, b * P:(b + 1) * P],
                                             w[:, k % per_unit, h * BANK:(h + 1) * BANK],
                                             start=(k == 0), stop=(k == nblocks - 1))
                        if b == TB - 1 and (k % per_unit == per_unit - 1 or k == nblocks - 1) and k < nblocks - 1:
                            used_up(last, unit)
                    last.then_inc(y_ps, 1)

            pe.wait_ge(probT_ok, TB * NQ)
            pe.wait_ge(o_ok, TB * PAIRS)

            def columns_attention():
                pe.wait_ge(rows_ok, 1)
                columns(2)

            project([("wout", 0), ("wout", 1)], 4, KD, lambda k: mixT[:, k, :], 2, {(1, 0): columns_attention})
            pe.wait_ge(red_ok, 3)
            def gu_products(j, t0, t1, before=None):
                w = slot(("gu", j // 2)).rearrange("p (f g k n) -> p f g k n", f=2, g=2, k=KD)
                for g in range(2):
                    for k in range(KD):
                        last = pe.matmul(ps[:, j % 4, g * SEQ + t0:g * SEQ + t1], w[:, j % 2, g, k, :],
                                         hT[:, k, t0:t1], start=(k == 0), stop=(k == KD - 1))
                        if before and (g, k) == (0, 0):
                            used_up(last, before)
                return last

            wait_landed(pe, ("gu", 0))
            for k in range(KD):
                wait_hT(2, 0, k)
            for j in range(4):
                if j == 2:
                    wait_landed(pe, ("gu", 1))
                if j == 3:
                    turn(2, 1, ("wout", 1))
                gu_products(j, 0, P)
            for k in range(KD):
                wait_hT(2, 1, k)
            for j in range(4):
                gu_products(j, P, SEQ, ("gu", 0) if j == 2 else None).then_inc(gu_ps, 1)
            for j in range(4, NF):
                if j % 2 == 0:
                    wait_landed(pe, ("gu", j // 2))
                pe.wait_ge(a_ok, j - 3)
                gu_products(j, 0, SEQ, None if j % 2 else ("gu", j // 2 - 1)).then_inc(gu_ps, 1)
                if j == 5:
                    pe.wait_ge(ada_acc, 8)
                    for i in range(2):
                        c = 3 * D + i * BANK
                        pe.matmul(ps[:, 4 + i, :], ones, acc[:, c:c + BANK], start=True, stop=True).then_inc(red_ps, 1)
            pe.wait_ge(ada_acc, 8 + 4)
            sum_rows(0, 7, ("gu", NF // 2 - 1))
            pe.wait_ge(red_ok, 5)

            def columns_ffn():
                pe.wait_ge(rows_ok, 2)
                pe.wait_ge(a_ok, NF)
                columns(0)

            project([("down", j) for j in range(-(-NF // 4))], 4, NF, lambda k: aT[:, k * SEQ:(k + 1) * SEQ], 3,
                    {(1, 0): columns_ffn}, a_ok)
            pe.wait_ge(red_ok, 6)
            def conv_products(i, t0, t1):
                j, part = i // 3, i % 3
                w = slot(("owin", i // 4)).rearrange("p (f k n) -> p f k n", f=4, k=KD)
                bank, c = (2 * (j % 2) + 1, 0) if part == 2 else (2 * (j % 2), part * SEQ)
                for k in range(KD):
                    last = pe.matmul(ps[:, bank, c + t0:c + t1], w[:, i % 4, k, :], hT[:, k, t0:t1],
                                     start=(k == 0), stop=(k == KD - 1))
                    if k == 0 and i % 4 == 0 and i >= 8:
                        used_up(last, ("owin", i // 4 - 1))
                return last

            wait_landed(pe, ("owin", 0))
            for k in range(KD):
                wait_hT(3, 0, k)
            for i in range(6):
                if i == 3:
                    turn(3, 1, ("down", -(-NF // 4) - 1))
                if i == 4:
                    wait_landed(pe, ("owin", 1))
                conv_products(i, 0, P)
            for k in range(KD):
                wait_hT(3, 1, k)
            for i in range(3 * KD):
                j = i // 3
                if i % 4 == 0 and i >= 8:
                    wait_landed(pe, ("owin", i // 4))
                if i % 3 == 0 and j >= 2:
                    pe.wait_ge(z_ok, j - 1)
                last = conv_products(i, P if i < 6 else 0, SEQ)
                if i % 3 == 2:
                    last.then_inc(conv_ps, 1)
                elif i == 3:
                    used_up(last, ("owin", 0))
            pe.wait_ge(ada_acc, 8 + 12)
            sum_rows(3 * D, 7, ("owin", 5))

            def gates_conv():
                pe.wait_ge(z_ok, KD)
                for i in range(4):
                    c = (5 if i >= 2 else 2) * D + (i % 2) * BANK
                    pe.matmul(ps[:, i, :], ones, acc[:, c:c + BANK], start=True, stop=True).then_inc(red_ps, 1)

            def columns_conv():
                pe.wait_ge(rows_ok, 3)
                pe.wait_ge(red_ok, 10)
                columns(0)

            project([("owout", 0), ("owout", 1)], 4, KD, lambda k: aT[:, k * SEQ:(k + 1) * SEQ], 4,
                    {(0, KD - 2): gates_conv, (1, 0): columns_conv}, z_ok)
            pe.wait_ge(red_ok, 11)
            router = vec[:, V_ROUTER:V_ROUTER + KD * E].rearrange("p (k e) -> p k e", e=E)
            for b in range(TB):
                if b == 1:
                    turn(4, 1)
                for k in range(KD):
                    wait_hT(4, b, k)
                    last = pe.matmul(ps[:, 0, b * E:(b + 1) * E], hT[:, k, b * P:(b + 1) * P], router[:, k, :],
                                     start=(k == 0), stop=(k == KD - 1))
                    if (b, k) == (0, 0):
                        used_up(last, ("owout", 1))
            last.then_inc(logit_ps, 1)
            pe.wait_ge(chosen_ok, 1)
            pe.wait_ge(late_in, 16)
            pe.matmul(ps[:, 1, 0:E], before, chosen[:, 0, :], start=True, stop=True)
            pe.matmul(ps[:, 1, E:2 * E], ones, chosen[:, 0, :], start=True, stop=False)
            pe.matmul(ps[:, 1, E:2 * E], before, chosen[:, 1, :], start=False, stop=True)
            pe.matmul(ps[0:1, 2, 0:E], ones[:, 0:1], chosen[:, 0, :], start=True, stop=False)
            pe.matmul(ps[0:1, 2, 0:E], ones[:, 0:1], chosen[:, 1, :], start=False, stop=True).then_inc(rank_ps, 1)

            def width_of(at):
                return pe.value_load(width_at[0:1, bass.ds(at, 1)], min_val=0, max_val=len(WIDTHS))

            def for_width(which, body):
                for i, width in enumerate(WIDTHS):
                    with pe.If(which == i):
                        body(width)

            def gather(width, e, before=None):
                pe.wait_ge(sel_ok, e + 1)
                n = max(width, 96)
                for j in range(4):
                    for i in range(2):
                        for b in range(TB):
                            last = pe.matmul(ps[:, j, i * SEQ:i * SEQ + n], xn[:, b, (2 * j + i) * P:(2 * j + i + 1) * P],
                                             sel[:, b, 0:n], start=(b == 0), stop=(b == TB - 1))
                            if (j, i, b) == (0, 0, 0) and before is not None:
                                last.then_inc(used[before], 1)
                    last.then_inc(gather_ps, 1)

            def landed_of(e, i):
                n = BASE + i
                pe.wait_ge(landed[n % RING], e * (16 * LAPS) + 16 * (n // RING + 1))
                return n % RING

            pe.wait_ge(width_ok, 1)
            for_width(width_of(0), lambda w: gather(w, 0))
            with pe.Fori(0, E) as e:
                width, next_width = width_of(e), width_of(e + 1)

                def is_wide(width):
                    return WIDTHS.index(width) >= WIDE

                def wide_steps(width):
                    return [(b, g, k) for b in range(2) for g in range(2) for k in range(KD)] if is_wide(width) else []

                def done_before(width, u):
                    if not is_wide(width) and any(n == 32 for _, n in BLOCKS[width]):
                        return [] if u % 2 else [u - 2, u - 1] if u else []
                    return [u - 1] if u else []

                def turn(width, u):
                    pe.wait_ge(e_a, e * GU_UNITS + u + 1)
                    if u >= 2:
                        pe.wait_ge(eT_ok, e * GU_UNITS + u - 1)
                    for b, (s0, n) in enumerate(BLOCKS[width]):
                        if n == 32 and u % 2 == 0:
                            continue
                        for c in range(2 if n == P else 1):
                            last = pe.transpose(ps[:, 6 + u % 2, b * 256 + c * P:b * 256 + (c + 1) * P],
                                                aT_e[:, u, b, c * P:(c + 1) * P], ident)
                    last.then_inc(eT_ps, 1)

                def gate_up(width):
                    for u in range(GU_UNITS):
                        landed_of(e, u)
                        if u >= 2:
                            pe.wait_ge(e_a, e * GU_UNITS + u - 1)
                        done, count = done_before(width, u), 0
                        for b, g, k in wide_steps(width):
                            w = ring[:, (BASE + u) % RING, k * 512 + g * 256 + b * P:k * 512 + g * 256 + (b + 1) * P]
                            last = pe.matmul(ps[:, 2 * (u % 2) + b, g * SEQ:g * SEQ + width], w, hTe[:, k, 0:width],
                                             start=(k == 0), stop=(k == KD - 1))
                            if count < len(done):
                                last.then_inc(used[(BASE + done[count]) % RING], 1)
                            count += 1
                        for b, (s0, n) in enumerate([] if is_wide(width) else BLOCKS[width]):
                            tiles = P // n
                            if tiles == 4 and u % 2 == 0:
                                continue
                            bank = 2 * (u % 2) + b
                            for k in range(KD):
                                for r in range(tiles):
                                    v = u if tiles < 4 else u - 1 + r // 2
                                    w = ring[:, (BASE + v) % RING, k * 512:(k + 1) * 512]
                                    to = ps[n * r:n * (r + 1), bank, :]
                                    if tiles > 1:
                                        w = w.rearrange("p (g c n) -> p g c n", g=2, c=2)[:, :, r % 2, :]
                                        to = to.rearrange("p (g c n) -> p g c n", g=2, c=2)[:, :, 0, :]
                                    last = pe.matmul(to, hTe[:, k, s0:s0 + n], w, start=(k == 0), stop=(k == KD - 1))
                                    if count < len(done):
                                        last.then_inc(used[(BASE + done[count]) % RING], 1)
                                    count += 1
                        last.then_inc(e_ps, 1)
                        if u == 1:
                            pe.wait_ge(comb_ok, e * 4 + 4)
                        if u and not is_wide(width):
                            turn(width, u - 1)
                        if u == 5:
                            pe.wait_ge(selw_ok, e + 1)
                            for b, (s0, n) in enumerate(BLOCKS[width]):
                                for t in range(TB):
                                    for r in range(P // n):
                                        last = pe.matmul(ps[n * r:n * (r + 1), 4, b * SEQ + t * P:b * SEQ + (t + 1) * P],
                                                         selw[:, t, s0:s0 + n], ident, start=True, stop=True)
                            last.then_inc(selT_ps, 1)

                def down(width):
                    pe.wait_ge(selT_ok, e + 1)
                    done, count = done_before(width, GU_UNITS), 0
                    for d in range(NFE // 4):
                        s = landed_of(e, GU_UNITS + d)
                        pe.wait_ge(e_a if is_wide(width) else eT_ok, e * GU_UNITS + 2 * d + 2)
                        w = ring[:, s, :].rearrange("p (f n) -> p f n", f=4)
                        for b, (s0, n) in enumerate(BLOCKS[width]):
                            tiles = P // n
                            if d == 0 and b == 1 and not is_wide(width):
                                pe.wait_ge(eT_ok, (e + 1) * GU_UNITS)
                            for h in range(2):
                                for f in range(4):
                                    j, r = 4 * d + f, f % tiles
                                    u = j // 2 if tiles < 4 else 2 * d + 1
                                    c = n * (f % 2 if tiles < 4 else f)
                                    a_T = aT_e[:, u, b, c:c + n]
                                    if is_wide(width):
                                        a_T = aT_e[:, j // 2, j % 2, s0:s0 + n]
                                    last = pe.matmul(ps[n * r:n * (r + 1), 4 + 2 * b + h, :], a_T,
                                                     w[:, f, h * BANK:(h + 1) * BANK],
                                                     start=(j < tiles), stop=(j >= NFE - tiles))
                                    if count < len(done):
                                        last.then_inc(used[(BASE + done[count]) % RING], 1)
                                    count += 1
                            if d < NFE // 4 - 1 and b == len(BLOCKS[width]) - 1:
                                last.then_inc(used[s], 1)
                            if d == 0 and b == 0 and not is_wide(width):
                                turn(width, GU_UNITS - 1)
                    last.then_inc(ye_ps, 1)
                    if is_wide(width):
                        pe.sem_inc(eT_ps, GU_UNITS)

                def combine(width):
                    for i in range(4):
                        for b in range(len(BLOCKS[width])):
                            last = pe.matmul(ps[:, 4 + i, :], selT[:, b, (i // 2) * P:(i // 2 + 1) * P],
                                             y_slot[:, b, (i % 2) * BANK:(i % 2 + 1) * BANK],
                                             start=(b == 0), stop=(b == len(BLOCKS[width]) - 1))
                        last.then_inc(comb_ps, 1)

                pe.wait_ge(hTe_act, e * 4 + 4)
                pe.wait_ge(hTe_dve, e * 4 + 4)
                for_width(width, gate_up)
                for_width(width, down)
                for_width(next_width, lambda w: gather(w, e + 1, (BASE + PER_EXPERT - 1) % RING))
                with pe.If(next_width == len(WIDTHS)):
                    pe.sem_inc(gather_ps, 4)
                pe.wait_ge(ye_act, e * 2 + 2)
                pe.wait_ge(ye_dve, e * 2 + 2)
                for_width(width, combine)


def kernel(**inputs):
    import concourse.bacc as bacc
    from concourse.bass_utils import run_bass_kernel_spmd

    a = {k: np.ascontiguousarray(v) for k, v in inputs.items()}
    f32 = np.float32

    stream = np.empty((UNITS, P, UNIT), f32)
    ada_w = a["ada_w"].reshape(2, KD, P, 6, D)
    cols = [h * HD + i for h in HEAD_ORDER for i in range(HD)]
    w_in = a["e_w_in"][0]
    w_in = np.concatenate([w_in[:, AW:AW + 2 * KW], w_in[:, cols], w_in[:, AW + 2 * KW:]], axis=1)
    w_out = np.concatenate([a["e_w_out"][0][cols], a["e_w_out"][0][AW:]], axis=0)

    def rows(w, j):
        return w[4 * j * P:4 * (j + 1) * P].reshape(-1, P, D).transpose(1, 0, 2).reshape(P, -1)

    def gate_up(g, u, j):
        gu = np.stack([g[:, 2 * j * P:2 * (j + 1) * P], u[:, 2 * j * P:2 * (j + 1) * P]])
        return gu.reshape(2, KD, P, 2, P)

    o_in = a["o_w_in"][0].reshape(KD, P, 3, KD, P).transpose(1, 3, 2, 0, 4).reshape(P, 6, UNIT)
    for n, (kind, *j) in enumerate(ORDER):
        if kind == "mod":
            half = ada_w[0, :, :, j[0] // 2, (j[0] % 2) * BANK:(j[0] % 2 + 1) * BANK]
            stream[n] = half.transpose(1, 0, 2).reshape(P, UNIT)
        elif kind == "win":
            stream[n] = w_in[:, BANK * j[0]:BANK * (j[0] + 1)].reshape(KD, P, BANK).transpose(1, 0, 2).reshape(P, UNIT)
        elif kind in ("ada0", "ada1"):
            layer = int(kind[3])
            s = j[0] + 2 * (layer == 0)
            stream[n] = ada_w[layer, 4 * j[1]:4 * j[1] + 4, :, s, :].transpose(1, 0, 2).reshape(P, UNIT)
        elif kind == "wout":
            stream[n] = rows(w_out, j[0])
        elif kind == "gu":
            stream[n] = gate_up(a["e_ffn_gate"][0], a["e_ffn_up"][0], j[0]).transpose(2, 3, 0, 1, 4).reshape(P, UNIT)
        elif kind == "down":
            r = rows(a["e_ffn_down"][0], j[0])
            stream[n, :, :r.shape[1]] = r
            stream[n, :, r.shape[1]:] = 0
        elif kind == "owin":
            stream[n] = o_in[:, j[0]]
        else:
            stream[n] = rows(a["o_w_out"][0], j[0])
    for e in range(E):
        for j in range(GU_UNITS):
            gu = gate_up(a["o_exp_gate"][0, e], a["o_exp_up"][0, e], j)
            stream[BASE + e * PER_EXPERT + j] = gu.transpose(2, 1, 0, 3, 4).reshape(P, UNIT)
        for j in range(NFE // 4):
            stream[BASE + e * PER_EXPERT + GU_UNITS + j] = rows(a["o_exp_down"][0, e], j)

    def by_channel(v):
        return np.moveaxis(v.reshape(*v.shape[:-1], KD, P), -1, 0)

    vecs = np.concatenate([
        by_channel(np.stack([a["c"][0], a["c_ctx"]])).transpose(0, 2, 1).reshape(P, -1),
        by_channel(a["ada_b"][0, :2 * D].reshape(2, D)).reshape(P, -1),
        by_channel(a["norm_w"][:, [0, 2]]).reshape(P, -1),
        by_channel(a["o_conv_w"][0]).reshape(P, -1),
        a["o_router"][0].reshape(KD, P, E).transpose(1, 0, 2).reshape(P, -1)], axis=1)
    assert vecs.shape[1] == V_END

    consts = np.concatenate([np.eye(P), np.ones((P, P)), np.tile(E - np.arange(E), (P, 1)),
                             np.arange(P)[:, None] % 32 == np.arange(2),
                             np.arange(P)[:, None] == 32 * np.arange(4)], axis=1).astype(f32)
    late = np.concatenate([np.tile(np.arange(SEQ), (P, 1)), np.triu(np.ones((P, P)), 1)], axis=1).astype(f32)
    pos = np.arange(SEQ)
    freq = (10000.0 ** (-np.arange(16, dtype=f32) / f32(16))).astype(f32)
    ang = np.stack([(pos // GRID_W).astype(f32)[:, None] * freq, (pos % GRID_W).astype(f32)[:, None] * freq], axis=1)
    cos, sin = np.cos(ang.astype(np.float64)), np.sin(ang.astype(np.float64))
    rope = np.stack([np.stack([cos, cos], axis=2), np.stack([-sin, sin], axis=2)]).reshape(2, TB, P, HD)
    rope = rope.transpose(2, 0, 1, 3).reshape(P, -1)
    rope = np.stack([rope * SCALE, rope], axis=1).reshape(P, -1).astype(f32)
    t = 2 * np.pi * np.outer(pos, pos) / SEQ
    g = 2 * np.pi * np.outer(np.arange(FG), np.arange(FG)) / FG
    over_t = np.concatenate([np.cos(t), np.sin(t)], axis=1).reshape(TB, P, 2 * SEQ).transpose(1, 0, 2) / SEQ ** 0.5
    over_g = np.concatenate([np.kron(np.eye(2), np.cos(g)), -np.kron(np.eye(2), np.sin(g))], axis=1) / FG ** 0.5
    dft = np.concatenate([over_t.reshape(P, -1), over_g], axis=1).astype(f32)
    swap = np.arange(HD).reshape(2, 2, 16)[:, ::-1].reshape(-1)
    gains = np.concatenate([a["e_q_gain"][0], a["e_q_gain"][0][swap], a["e_k_gain"][0], a["e_k_gain"][0][swap]])[None]

    arrays = {
        "stream": stream, "x_in": a["x"][0], "ctx_in": a["ctx"][0], "vecs": vecs, "consts": consts,
        "rope": rope, "dft": dft, "gains": gains, "ada_b": a["ada_b"], "norm_w": a["norm_w"].reshape(8, D),
        "late": late,
    }
    arrays = {k: np.ascontiguousarray(v) for k, v in arrays.items()}
    nc = bacc.Bacc("TRN2", target_bir_lowering=False, num_devices=1)
    args = [nc.dram_tensor(k, v.shape, F32, kind="ExternalInput").ap() for k, v in arrays.items()]
    out = nc.dram_tensor("out", (SEQ, D), F32, kind="ExternalOutput").ap()
    build(nc, *args, out)
    r = run_bass_kernel_spmd(nc, [arrays], core_ids=[0])
    return r.results[0]["out"].reshape(1, SEQ, D)
```
